# Optimizing a Trainium2 kernel written in Bass

```python
import jax, jax.numpy as jnp
from jax import lax
import numpy as np

D_MODEL = 1024
BATCH = 1
SEQ = 1024
DEPTH = 2

PLE_DIM = 256
RET_HEADS = 6
RET_HEAD_DIM = 64
RET_WIDTH = RET_HEADS * RET_HEAD_DIM
POOL_WINDOWS = (2, 4, 8, 16)
POOL_GROUPS = len(POOL_WINDOWS)
POOL_GROUP_DIM = 64
POOL_WIDTH = POOL_GROUPS * POOL_GROUP_DIM
MLSTM_HEADS = 4
MLSTM_HEAD_DIM = 96
MLSTM_WIDTH = MLSTM_HEADS * MLSTM_HEAD_DIM
MLSTM_CONV = 4
MIX_WIDTH = RET_WIDTH + POOL_WIDTH + MLSTM_WIDTH
IN_WIDTH = 4 * RET_WIDTH + POOL_WIDTH + 4 * MLSTM_WIDTH + 2 * MLSTM_HEADS
CHUNK = 128
D_FF = -(-8 * D_MODEL // (3 * 256)) * 256
ROPE_BASE = 10000.0
EPS = 1e-6

kernel_name = "hybrid_retention_pool_mlstm_block"

def rmsnorm(x, g):
    xf = x.astype(jnp.float32)
    y = xf * lax.rsqrt(jnp.mean(xf * xf, axis=-1, keepdims=True) + EPS)
    return (y * g.astype(jnp.float32)).astype(x.dtype)

def head_norm(h, g):
    b, s, nh, d = h.shape
    mu = jnp.mean(h, axis=-1, keepdims=True)
    hc = h - mu
    var = jnp.mean(hc * hc, axis=-1, keepdims=True)
    y = (hc * lax.rsqrt(var + EPS)).reshape(b, s, nh * d)
    return y * g.astype(jnp.float32)

def rope(x, pos):
    half = x.shape[-1] // 2
    inv = ROPE_BASE ** (-jnp.arange(half, dtype=jnp.float32) / half)
    ang = pos.astype(jnp.float32)[..., None] * inv
    cos = jnp.cos(ang)[:, :, None, :]
    sin = jnp.sin(ang)[:, :, None, :]
    x1, x2 = x[..., :half], x[..., half:]
    return jnp.concatenate([x1 * cos - x2 * sin, x1 * sin + x2 * cos], axis=-1)

def to_chunks(x):
    b, s, nh, d = x.shape
    return x.reshape(b, s // CHUNK, CHUNK, nh, d).transpose(0, 3, 1, 2, 4)

def from_chunks(y):
    b, nh, nc, c, d = y.shape
    return y.transpose(0, 2, 3, 1, 4).reshape(b, nc * c, nh, d)

def causal_conv(x, w, bias):
    k, c = w.shape
    y = lax.conv_general_dilated(
        x, w[:, None, :].astype(x.dtype), window_strides=(1,),
        padding=((k - 1, 0),), dimension_numbers=("NWC", "WIO", "NWC"),
        feature_group_count=c)
    return y + bias.astype(x.dtype)

def retention(q, k, v, g, pos, gn_gain):
    f32 = jnp.float32
    b, s, _ = q.shape
    nh, d = RET_HEADS, RET_HEAD_DIM
    qh = rope(q.reshape(b, s, nh, d).astype(f32), pos)
    kh = rope(k.reshape(b, s, nh, d).astype(f32), pos) * (d ** -0.5)
    vh = v.reshape(b, s, nh, d).astype(f32)
    log_gamma = jnp.log1p(-(2.0 ** (-5.0 - jnp.arange(nh, dtype=f32))))
    qc, kc, vc = to_chunks(qh), to_chunks(kh), to_chunks(vh)
    idx = jnp.arange(CHUNK, dtype=f32)
    rel = idx[:, None] - idx[None, :]
    decay = jnp.where(rel >= 0, jnp.exp(log_gamma[:, None, None] * jnp.maximum(rel, 0.0)), 0.0)
    scores = jnp.einsum('bhncd,bhnsd->bhncs', qc, kc) * decay[None, :, None]
    y_intra = jnp.einsum('bhncs,bhnse->bhnce', scores, vc)
    zeta = jnp.exp(log_gamma[:, None] * (CHUNK - 1 - idx))
    kv = jnp.einsum('bhncd,bhnce->bhnde', kc * zeta[None, :, None, :, None], vc)
    chunk_decay = jnp.exp(log_gamma * CHUNK)[None, :, None, None]

    def step(r, kv_n):
        return chunk_decay * r + kv_n, r

    _, r_prev = lax.scan(step, jnp.zeros((b, nh, d, d), f32), jnp.moveaxis(kv, 2, 0))
    r_prev = jnp.moveaxis(r_prev, 0, 2)
    xi = jnp.exp(log_gamma[:, None] * (idx + 1.0))
    y_cross = jnp.einsum('bhncd,bhnde->bhnce', qc, r_prev) * xi[None, :, None, :, None]
    y = head_norm(from_chunks(y_intra + y_cross), gn_gain)
    return (jax.nn.silu(g.astype(f32)) * y).astype(q.dtype)

def pool_mix(u, w_pool, pool_scale):
    f32 = jnp.float32
    b, s, _ = u.shape
    uf = u.astype(f32)
    csum = jnp.pad(lax.cumsum(uf, axis=1), ((0, 0), (1, 0), (0, 0)))
    t1 = jnp.arange(1, s + 1, dtype=f32)
    outs = []
    for gi, w in enumerate(POOL_WINDOWS):
        lo, hi = gi * POOL_GROUP_DIM, (gi + 1) * POOL_GROUP_DIM
        cs = csum[:, :, lo:hi]
        upper = cs[:, 1:]
        lower = jnp.pad(cs[:, :s + 1 - w], ((0, 0), (w - 1, 0), (0, 0)))
        count = jnp.minimum(t1, float(w))[None, :, None]
        outs.append((upper - lower) / count - uf[:, :, lo:hi])
    pooled = jnp.stack(outs, axis=2)
    mixed = jnp.einsum('bsgc,gcd->bsgd', pooled, w_pool.astype(f32)).reshape(b, s, POOL_WIDTH)
    return (mixed * pool_scale.astype(f32)).astype(u.dtype)

def mlstm(q, k, v, o, i_pre, f_pre, conv_w, conv_b, b_i, b_f, gn_gain):
    f32 = jnp.float32
    b, s, _ = q.shape
    nh, d = MLSTM_HEADS, MLSTM_HEAD_DIM
    qk = jax.nn.silu(causal_conv(jnp.concatenate([q, k], axis=-1).astype(f32), conv_w.astype(f32), conv_b))
    qh = qk[..., :MLSTM_WIDTH].reshape(b, s, nh, d) * (d ** -0.5)
    kh = qk[..., MLSTM_WIDTH:].reshape(b, s, nh, d)
    vh = v.reshape(b, s, nh, d).astype(f32)
    log_i = i_pre.astype(f32) + b_i.astype(f32)
    log_f = jax.nn.log_sigmoid(f_pre.astype(f32) + b_f.astype(f32))
    nc = s // CHUNK
    qc, kc, vc = to_chunks(qh), to_chunks(kh), to_chunks(vh)
    li = log_i.reshape(b, nc, CHUNK, nh).transpose(0, 3, 1, 2)
    lf = log_f.reshape(b, nc, CHUNK, nh).transpose(0, 3, 1, 2)
    bcum = lax.cumsum(lf, axis=3)
    b_last = bcum[..., -1]
    causal = jnp.tril(jnp.ones((CHUNK, CHUNK), dtype=bool))
    log_d = jnp.where(causal, bcum[..., :, None] - bcum[..., None, :] + li[..., None, :], -jnp.inf)
    log_w = b_last[..., None] - bcum + li
    a = jnp.max(log_w, axis=-1)
    kw = kc * jnp.exp(log_w - a[..., None])[..., None]
    kv_loc = jnp.einsum('bhncd,bhnce->bhnde', kw, vc)
    n_loc = jnp.sum(kw, axis=3)

    def step(carry, xs):
        c_st, n_st, m_st = carry
        kv_n, n_n, a_n, bl_n = xs
        m_new = jnp.maximum(bl_n + m_st, a_n)
        s_old = jnp.exp(bl_n + m_st - m_new)
        s_new = jnp.exp(a_n - m_new)
        c_new = s_old[..., None, None] * c_st + s_new[..., None, None] * kv_n
        n_new = s_old[..., None] * n_st + s_new[..., None] * n_n
        return (c_new, n_new, m_new), (c_st, n_st, m_st)

    init = (jnp.zeros((b, nh, d, d), f32), jnp.zeros((b, nh, d), f32), jnp.zeros((b, nh), f32))
    xs = (jnp.moveaxis(kv_loc, 2, 0), jnp.moveaxis(n_loc, 2, 0), jnp.moveaxis(a, 2, 0), jnp.moveaxis(b_last, 2, 0))
    _, (c_prev, n_prev, m_prev) = lax.scan(step, init, xs)
    c_prev = jnp.moveaxis(c_prev, 0, 2)
    n_prev = jnp.moveaxis(n_prev, 0, 2)
    m_prev = jnp.moveaxis(m_prev, 0, 2)
    log_inter = bcum + m_prev[..., None]
    m_row = jnp.maximum(log_inter, jnp.max(log_d, axis=-1))
    sc = jnp.einsum('bhncd,bhnsd->bhncs', qc, kc) * jnp.exp(log_d - m_row[..., None])
    inter = jnp.exp(log_inter - m_row)
    num = jnp.einsum('bhncs,bhnse->bhnce', sc, vc) + inter[..., None] * jnp.einsum('bhncd,bhnde->bhnce', qc, c_prev)
    den = jnp.sum(sc, axis=-1) + inter * jnp.einsum('bhncd,bhnd->bhnc', qc, n_prev)
    den = jnp.maximum(jnp.abs(den), jnp.exp(-m_row))
    h = head_norm(from_chunks(num / den[..., None]), gn_gain)
    return (jax.nn.sigmoid(o.astype(f32)) * h).astype(q.dtype)

def hybrid_layer(x, p_i, positions, norm_mix, w_in, ret_gn, pool_w, pool_scale,
                 conv_w, conv_b, b_igate, b_fgate, mlstm_gn, w_out, norm_ffn,
                 w_gate_up, w_down, norm_ple, w_ple_gate, w_ple_proj):
    h = rmsnorm(x, norm_mix)
    z = h @ w_in
    sizes = [RET_WIDTH] * 4 + [POOL_WIDTH] + [MLSTM_WIDTH] * 4 + [MLSTM_HEADS] * 2
    offs = np.cumsum(sizes)[:-1].tolist()
    (rq, rk, rv, rg, pu, mq, mk, mv, mo, mi, mf) = jnp.split(z, offs, axis=-1)
    y_ret = retention(rq, rk, rv, rg, positions, ret_gn)
    y_pool = pool_mix(pu, pool_w, pool_scale)
    y_ml = mlstm(mq, mk, mv, mo, mi, mf, conv_w, conv_b, b_igate, b_fgate, mlstm_gn)
    x = x + jnp.concatenate([y_ret, y_pool, y_ml], axis=-1) @ w_out
    h = rmsnorm(x, norm_ffn)
    gu = h @ w_gate_up
    x = x + (jax.nn.silu(gu[..., :D_FF]) * gu[..., D_FF:]) @ w_down
    hp = rmsnorm(x, norm_ple)
    x = x + jax.nn.sigmoid(hp @ w_ple_gate) * (p_i @ w_ple_proj)
    return x

def setup_inputs(seed: int = 0) -> dict:
    key = jax.random.key(seed)
    ks = jax.random.split(key, 24)
    f32 = jnp.float32

    def nrm(k, shape, scale):
        return jax.random.normal(k, shape, f32) * scale

    def gain(k, shape):
        return 1.0 + 0.05 * jax.random.normal(k, shape, f32)

    return {
        "x": nrm(ks[0], (BATCH, SEQ, D_MODEL), 1.0),
        "p": nrm(ks[1], (DEPTH, BATCH, SEQ, PLE_DIM), 1.0),
        "positions": jnp.broadcast_to(jnp.arange(SEQ, dtype=jnp.int32), (BATCH, SEQ)),
        "norm_mix": gain(ks[2], (DEPTH, D_MODEL)),
        "w_in": nrm(ks[3], (DEPTH, D_MODEL, IN_WIDTH), D_MODEL ** -0.5),
        "ret_gn": gain(ks[4], (DEPTH, RET_WIDTH)),
        "pool_w": nrm(ks[5], (DEPTH, POOL_GROUPS, POOL_GROUP_DIM, POOL_GROUP_DIM), POOL_GROUP_DIM ** -0.5),
        "pool_scale": gain(ks[6], (DEPTH, POOL_WIDTH)),
        "conv_w": nrm(ks[7], (DEPTH, MLSTM_CONV, 2 * MLSTM_WIDTH), MLSTM_CONV ** -0.5),
        "conv_b": nrm(ks[8], (DEPTH, 2 * MLSTM_WIDTH), 0.02),
        "b_igate": nrm(ks[9], (DEPTH, MLSTM_HEADS), 0.1),
        "b_fgate": jnp.broadcast_to(jnp.linspace(3.0, 6.0, MLSTM_HEADS, dtype=f32), (DEPTH, MLSTM_HEADS)) + nrm(ks[10], (DEPTH, MLSTM_HEADS), 0.1),
        "mlstm_gn": gain(ks[11], (DEPTH, MLSTM_WIDTH)),
        "w_out": nrm(ks[12], (DEPTH, MIX_WIDTH, D_MODEL), MIX_WIDTH ** -0.5),
        "norm_ffn": gain(ks[13], (DEPTH, D_MODEL)),
        "w_gate_up": nrm(ks[14], (DEPTH, D_MODEL, 2 * D_FF), D_MODEL ** -0.5),
        "w_down": nrm(ks[15], (DEPTH, D_FF, D_MODEL), D_FF ** -0.5),
        "norm_ple": gain(ks[16], (DEPTH, D_MODEL)),
        "w_ple_gate": nrm(ks[17], (DEPTH, D_MODEL, D_MODEL), D_MODEL ** -0.5),
        "w_ple_proj": nrm(ks[18], (DEPTH, PLE_DIM, D_MODEL), PLE_DIM ** -0.5),
        "norm_final": gain(ks[19], (D_MODEL,)),
    }

def reference(x, p, positions, norm_mix, w_in, ret_gn, pool_w, pool_scale,
              conv_w, conv_b, b_igate, b_fgate, mlstm_gn, w_out, norm_ffn,
              w_gate_up, w_down, norm_ple, w_ple_gate, w_ple_proj, norm_final):
    for i in range(DEPTH):
        x = hybrid_layer(x, p[i], positions, norm_mix[i], w_in[i], ret_gn[i],
                         pool_w[i], pool_scale[i], conv_w[i], conv_b[i],
                         b_igate[i], b_fgate[i], mlstm_gn[i], w_out[i],
                         norm_ffn[i], w_gate_up[i], w_down[i], norm_ple[i],
                         w_ple_gate[i], w_ple_proj[i])
    return rmsnorm(x, norm_final)


_drawn_inputs = setup_inputs


def setup_inputs(seed=0):
    import zlib

    import numpy as np

    out = dict(_drawn_inputs(seed))
    spreads = {}
    factors = {'conv_b': 4.099,
     'b_igate': 200.0,
     'mlstm_gn': 2.725,
     'norm_ple': 5.67,
     'ret_gn': 3.118,
     'pool_scale': 2.94}
    for name, (base, spread) in spreads.items():
        noise = np.random.default_rng([zlib.crc32(name.encode()), seed]).standard_normal(out[name].shape)
        drawn = base * np.exp(spread * noise) if base else spread * noise
        out[name] = __import__('jax').numpy.asarray(drawn.astype(out[name].dtype))
    for name, factor in factors.items():
        out[name] = (out[name] * factor).astype(out[name].dtype)
    return out
```

```python
from contextlib import ExitStack

import numpy as np

import concourse.bass as bass
from concourse import mybir

F32 = mybir.dt.float32
F32R = mybir.dt.float32r
I32 = mybir.dt.int32
ACT = mybir.ActivationFunctionType
ALU = mybir.AluOpType
AX = mybir.AxisListType

P = 128
D = 1024
S = 1024
HALF = 512
DEPTH = 2
KC = D // P
PLE = 256
RH, RD = 6, 64
RW = RH * RD
PAIRS = RW // P
PW = 256
MH, MD = 4, 96
MW = MH * MD
MC = MW // P
CONV = 4
CHUNK = 128
NCH = S // CHUNK
DFF = 2816
FG = DFF // (2 * P)
EPS = 1e-6
MSCALE = float(MD) ** -0.5
RSCALE = float(RD) ** -0.5

U_GATES, U_MQ, U_MK, U_MV, U_MO, U_RG, U_POOL, U_RET, U_OUT, U_FFN = 0, 1, 4, 7, 10, 13, 16, 18, 27, 35
U_PROJ = U_FFN + 6 * FG
U_GATE = U_PROJ + 2
UNITS = U_GATE + 8
RING = 3
assert UNITS % RING == 0

BLOCKS = [(0, 0, 0, 96), (1, 0, 96, 128), (1, 1, 0, 64), (2, 1, 64, 128), (2, 2, 0, 32), (3, 2, 32, 128)]
NB = len(BLOCKS)
MIX_ORDER = [5, 6, 7, 3, 4, 0, 1, 2]

C_ID, C_ONE, C_PERM, C_CEN, C_MEAN, C_NEG = [i * P for i in range(6)]
C_DEC = 6 * P
C_XI = C_DEC + RH * P
C_SEL = C_XI + PAIRS * P
C_ZETA = C_SEL + MH * P
C_GAM = C_ZETA + RH
C_FREQ = C_GAM + PAIRS
C_INVC = C_FREQ + 1
C_INVW = C_INVC + 2 * 16
C_BLK = C_INVW + 2
C_ALL = C_BLK + NB

A_FFN, A_PLE, A_NEXT = 0, 8, 16
A_CW = 24
A_CB = A_CW + 6 * CONV
A_GB = A_CB + 6
A_RG = A_GB + 1
A_PS = A_RG + PAIRS
A_MG = A_PS + 2
A_PW = A_MG + MC
A_ALL = A_PW + 2 * P


def macro_schedule():
    m = [("unit", u) for u in range(U_MO)] + [("ml_cols",)]
    for n in range(NCH):
        m += [("ml_a", n), ("half", U_MO + n, 0), ("ml_b", n), ("half", U_MO + n, 1)]
    m += [("gate_funcs",), ("unit", U_RET), ("ml_fin",), ("unit", U_RET + 1), ("pool",), ("unit", U_RET + 2)]
    for p in range(PAIRS):
        steps = ["rope", "turn", "scores", "state", "ret_y", "centre", "spread"]
        halves = [(U_RET + 3 * (p + 1) + i // 2, i % 2) for i in range(6)] if p < PAIRS - 1 else []
        for i, s in enumerate(steps):
            m.append((s, p))
            if i < len(halves):
                m.append(("half", *halves[i]))
    m += [("mix_split",), ("out_units",), ("norm", 0), ("p_split",), ("ffn",),
          ("ple_proj",), ("ple_gate",), ("norm", 2)]
    return m


MACRO = macro_schedule()


def unit_fills(u):
    return 8 if is_wide(u) else 2


def is_wide(u):
    if U_FFN + 4 <= u < U_PROJ - 2:
        return (u - U_FFN - 4) % 6 >= 4
    return U_PROJ - 2 <= u < U_GATE


FILL0 = [sum(unit_fills(v) for v in range(u)) for u in range(UNITS + 1)]
FILLS = FILL0[UNITS]
FILLS_TOLD = FILLS - UNITS

STAGE_FILLS = {
    "ml_cols": lambda *a: [(("tt", b), b) for b in range(4)] + [(("so",), 0)],
    "ml_a": lambda n: [(("tk", n), 0), (("tv", n), 1), (("mb", n), 2), (("ms", n), 3)],
    "ml_b": lambda n: [(("num", n), 0), (("int", n), 1)] + ([(("kv0", n), 2), (("kv1", n), 3)] if n < NCH - 1 else []),
    "ml_fin": lambda *a: [(("yt", j, h), (2 * j + h) % 4) for j in range(MC) for h in range(2)],
    "pool": lambda *a: [(("pm", j, h), 2 * j + h) for j in range(2) for h in range(2)],
    "rope": lambda p: [(("pq", p, 0), 0), (("pq", p, 1), 1), (("pk", p, 0), 2), (("pk", p, 1), 3)],
    "turn": lambda p: [(("vt", p, 0), 0), (("vt", p, 1), 1), (("kz", p, 0), 2), (("kz", p, 1), 3)],
    "scores": lambda p: [(("rs", p, e, h), 2 * e + h) for e in range(2) for h in range(2)],
    "state": lambda p: [(("rkv", p), 0)],
    "ret_y": lambda p: [(("ry", p, h), 1 + h) for h in range(2)],
    "centre": lambda p: [(("rc", p, 0), 3), (("rc", p, 1), 0)],
    "spread": lambda p: [(("rv", p, h), 1 + h) for h in range(2)],
}


def norm_fills(i):
    return [(("sum", i, 0), 0), (("sum", i, 1), 1), (("row", i, 0), 2), (("row", i, 1), 3)]


def plan_aux():
    table, order, per_bank = {}, 0, [0] * 4
    for item in MACRO:
        if item[0] == "norm":
            fills = norm_fills(item[1])
        elif item[0] == "ple_proj":
            fills = norm_fills(1)
        elif item[0] in STAGE_FILLS:
            fills = STAGE_FILLS[item[0]](*item[1:])
        else:
            continue
        for name, bank in fills:
            table[name] = (bank, order, per_bank[bank])
            order += 1
            per_bank[bank] += 1
    return table, order, per_bank


AUX, AUX_FILLS, AUX_PER_BANK = plan_aux()
VEC_STEPS = 354


PRE_VEC = 20


class LoopValues:

    def __init__(self, i):
        self.units, self.acts, self.told = i * 12, i * 8, i * 36
        self.fills = i * 12


class Signal:

    def __init__(self, sem, per_layer, start=0):
        self.sem, self.per_layer, self.start = sem, per_layer, start

    def at(self, layer, k):
        return layer * self.per_layer + (k + self.start)


def build(nc, w_d, x_d, p_d, pos_d, const_d, par_d, gain0_d, out_d):
    spill_d = nc.dram_tensor("x_spill", (P, KC, S), F32, kind="Internal").ap()
    with ExitStack() as ctx:
        def sb(name, shape, dt=F32):
            return ctx.enter_context(nc.sbuf_tensor(name, shape, dt))[:]

        def sem(name):
            return ctx.enter_context(nc.semaphore(name))

        hh = sb("h_hi", [P, KC, S], F32R)
        hl = sb("h_lo", [P, KC, S], F32R)
        raw = sb("w_raw", [P, RING, 1024])
        whi = sb("w_hi", [P, RING, 1024], F32R)
        wlo = sb("w_lo", [P, RING, 1024], F32R)
        const = sb("const", [P, C_ALL])
        par = sb("par", [P, A_ALL])
        gain0 = sb("gain0", [P, KC])
        cosT = sb("cosT", [P, S])
        sinT = sb("sinT", [P, S])
        rows = sb("rows", [P, 2, S])
        small = sb("small", [P, 64])
        zero1 = sb("zero1", [P, 1])
        XB = 4 * KC * S
        WB = 30720
        arena_at = -(-nc.sbuf_base // 64) * 64
        sb("arena", [P, (2 * XB + WB + 64) // 4])
        x_at, mix_at, w_at = arena_at, arena_at + XB, arena_at + 2 * XB

        def at(name, offset, shape, dt=F32):
            return nc.alloc_sbuf_tensor_at(name, shape, dt, offset=offset)[:]

        x = at("x", x_at, [P, KC, S])
        mix = at("mix", mix_at, [P, KC, S])
        ahi = at("act_hi", mix_at, [P, 2, 2, S], F32R)
        alo = at("act_lo", mix_at + 4 * 4 * S, [P, 2, 2, S], F32R)
        pp = at("ple_in", mix_at, [P, KC, S])
        qk = at("ml_qk", x_at, [P, 6, S])
        gw = 4 * S
        t_at = x_at + 6 * gw
        dmat = at("ml_d", t_at, [P, MH, P])
        smat = at("ml_s", t_at + 2048, [P, MH, P])
        num = at("ml_num", t_at + 4096, [P, MH, MD + 1])
        tnum = at("ml_tmp", t_at + 5664, [P, MH, MD + 1])
        pool_t = at("pool_t", t_at, [P, 2, S])
        vm = at("ml_v", w_at, [P, NCH, MW])
        convraw = at("conv_raw", w_at + 12288, [P, 2, S + CONV - 1])
        kw = at("ml_kw", w_at + 12288, [P, NB, P])
        cst = at("ml_c", w_at + 15360, [P, 2, NB, MD + 1])
        tt = at("ml_cols", w_at + 20032, [P, NCH, 5, MH])
        so6 = at("ml_so", w_at + 20672, [P, NB, NCH])
        vx = at("ml_vx", w_at + 20864, [P, 2, MH, MD + 1])
        km = at("ml_km", w_at + 23968, [P, 2, NB, P])
        rqkv = at("ret_qkv", x_at, [P, 2, 3, S])
        sc1 = at("ret_s1", t_at, [P, NCH, P])
        rst = at("ret_state", t_at + gw, [P, NCH, RD])
        rw = [at(f"ret_t{i}", w_at + gw * i, [P, S]) for i in range(7)]
        sqr = at("squares", w_at, [P, 2, HALF])
        nt = at("normed", w_at, [P, 2, HALF])
        silu_g = at("silu_g", w_at, [P, 2, HALF])
        acc = at("square_sum", w_at + 4096, [P, 2, HALF])
        act_t = at("act", w_at + 4096, [P, 2, HALF])
        diag = at("diag", w_at + 8192, [P, 4, P])
        rstd = at("rstd", w_at + 10240, [P, 2, HALF])
        praw = at("p_raw", w_at + 22528, [P, 2, S])
        phi = at("p_hi", w_at + 14336, [P, 2, S], F32R)
        plo = at("p_lo", w_at + 22528, [P, 2, S], F32R)
        psg = at("ple_sig", w_at + 14336, [P, 2, HALF])
        pt = at("ple_t", w_at + 14336 + 4096, [P, 2, HALF])
        ang = at("ang", mix_at, [P, 5, S])
        posi = at("posi", mix_at + 5 * gw, [P, S], I32)

        proj = ctx.enter_context(nc.psum_tensor("proj", [P, 4, HALF], F32))
        aux = ctx.enter_context(nc.psum_tensor("aux", [P, 4, HALF], F32))

        ident = const[:, C_ID:C_ID + P]
        ones = const[:, C_ONE:C_ONE + P]
        eps_c, one_c, zero_c = small[:, 0:1], small[:, 1:2], small[:, 2:3]
        mprev = small[0:MH, 8:8 + NCH]
        rt_c, rc_c = small[:, 16:24], small[:, 24:32]
        den_c, rden_c, mean_c = small[:, 32:36], small[:, 36:40], small[:, 40:44]
        stat = sb("stat", [P, 2, NCH, MH])
        tmp16 = sb("tmp16", [P, 16])

        const_landed, x_landed, pos_landed = sem("const_landed"), sem("x_landed"), sem("pos_landed")
        par_landed, spilled, reloaded, p_landed = sem("par_landed"), sem("spilled"), sem("reloaded"), sem("p_landed")
        out_stored = sem("out_stored")
        raw_landed = [sem(f"raw_landed{r}") for r in range(RING)]
        w_hi_made = sem("w_hi_made")
        weights_ready = Signal(sem("weights_ready"), UNITS, RING)
        unit_done = Signal(sem("unit_done"), UNITS, RING)
        fill_done = Signal(sem("fill_done"), FILLS_TOLD)
        emptied = [Signal(sem(f"proj_emptied{b}"), len(range(b, FILLS, 4)), 1) for b in range(4)]
        aux_done = Signal(sem("aux_done"), AUX_FILLS, 4)
        aux_emptied = [Signal(sem(f"aux_emptied{b}"), AUX_PER_BANK[b], 1) for b in range(4)]
        sq_made = Signal(sem("sq_made"), 48, 16)
        sq_added = Signal(sem("sq_added"), 48, 16)
        diag_made = Signal(sem("diag_made"), 6, 2)
        normed = Signal(sem("normed"), 48, 16)
        h_hi = Signal(sem("h_hi_made"), 64, 16)
        h_ready = Signal(sem("h_ready"), 64, 16)
        silu_made = Signal(sem("qk_ready"), 6)
        row_act = Signal(sem("row_funcs"), 5)
        d_exp = Signal(sem("d_exp"), NCH)
        gated = Signal(sem("gate_funcs"), 6)
        ml_rt = Signal(sem("ml_root"), 1)
        ret_sq = Signal(sem("ret_squares"), 2 * PAIRS)
        p_hi_made = Signal(sem("p_hi_made"), 2)
        p_ready = Signal(sem("p_ready"), 2)
        act_hi_made = Signal(sem("act_hi_made"), 4 * FG)
        act_ready = Signal(sem("act_ready"), 4 * FG)
        rc_sig = Signal(sem("token_rstd"), 6, 2)
        result = sem("result")
        x_ple = Signal(sem("x_ple"), 16)
        vec_step = Signal(sem("vec_step"), VEC_STEPS)
        pre_vec, pre_act = sem("pre_vec"), sem("pre_act")

        block = ctx.enter_context(nc.Block())
        marks = {}

        def bank(u, k):
            return (FILL0[u] + k) % 4

        def filled(u, k):
            return unit_done.sem if k == unit_fills(u) - 1 else fill_done.sem

        def filled_at(L, u, k, more=0, more_units=0):
            if k == unit_fills(u) - 1:
                return unit_done.at(L, more_units + (u + 1))
            return fill_done.at(L, more + (FILL0[u] - u + k + 1))

        def emptied_at(L, u, k, more=0):
            return emptied[bank(u, k)].at(L, more + ((FILL0[u] + k) // 4 + 1))

        def free_at(L, u, k, more=0):
            return emptied[bank(u, k)].at(L, more + (FILL0[u] + k) // 4)

        def aux_at(L, name):
            return aux_done.at(L, AUX[name][1] + 1)

        def aux_read(name):
            return aux_emptied[AUX[name][0]].sem

        def aux_read_at(L, name):
            return aux_emptied[AUX[name][0]].at(L, AUX[name][2] + 1)

        def aux_free_at(L, name):
            return aux_emptied[AUX[name][0]].at(L, AUX[name][2])

        def mark_at(L, name):
            return vec_step.at(L, marks[name])

        def pbank(u, k):
            return proj[:, (FILL0[u] + k) % 4, :]

        def abank(name):
            return aux[:, AUX[name][0], :]

        def hs(half):
            return slice(HALF * half, HALF * half + HALF)

        @block.vector
        def _(v):
            steps = [0]

            def count(mark=None):
                steps[0] += 1
                if mark is not None:
                    marks[mark] = steps[0]

            def step_at(L, mark=None):
                count(mark)
                return vec_step.at(L, steps[0])

            def norm_rows(L, base, i):
                for h in range(2):
                    if i is None:
                        v.wait_ge(aux_emptied[h].sem, 1)
                    else:
                        v.wait_ge(aux_read(("sum", i, h)), aux_read_at(L, ("sum", i, h)))
                    v.reciprocal(rc_c[:, 4 * h:4 * h + 4], rt_c[:, 4 * h:4 * h + 4]).then_inc(rc_sig.sem, 1)
                    v.wait_ge(rc_sig.sem, rc_sig.at(L, base + h + 1))
                    if h == 1:
                        if i is None:
                            v.wait_ge(aux_done.sem, 3)
                        else:
                            v.wait_ge(aux_done.sem, aux_at(L, ("row", i, 0)))
                    v.tensor_tensor(diag[:, :, :], ident.unsqueeze(1).to_broadcast([P, 4, P]),
                                    rc_c[:, 4 * h:4 * h + 4].unsqueeze(2).to_broadcast([P, 4, P]),
                                    ALU.mult).then_inc(diag_made.sem, 1)

            def norm_apply(L, base, hbase, gains, i):
                for j in range(16 + 1):
                    if j < 16:
                        h, c = divmod(j, 8)
                        if c == 0:
                            if i is None:
                                v.wait_ge(aux_emptied[2 + h].sem, 1)
                            else:
                                v.wait_ge(aux_read(("row", i, h)), aux_read_at(L, ("row", i, h)))
                        v.scalar_tensor_tensor(nt[:, j % 2, :], x[:, c, hs(h)], gains[:, c:c + 1], rstd[:, h, :],
                                               ALU.mult, ALU.mult).then_inc(normed.sem, 1)
                    if j >= 1:
                        h, c = divmod(j - 1, 8)
                        v.wait_ge(h_hi.sem, h_hi.at(L, hbase + j))
                        v.wait_ge(normed.sem, normed.at(L, base + j))
                        v.tensor_tensor(hl[:, c, hs(h)], nt[:, (j - 1) % 2, :], hh[:, c, hs(h)].bitcast(F32),
                                        ALU.subtract).then_inc(h_ready.sem, 1)
                    if 1 <= j < 15:
                        v.wait_ge(h_ready.sem, h_ready.at(L, hbase + j))

            def add_square(L, base, j):
                c, h = divmod(j, 2)
                v.wait_ge(sq_made.sem, sq_made.at(L, base + j + 1))
                if c == 0:
                    v.tensor_copy(acc[:, h, :], sqr[:, j % 2, :]).then_inc(sq_added.sem, 1)
                else:
                    v.wait_ge(sq_added.sem, sq_added.at(L, base + j - 1))
                    v.tensor_tensor(acc[:, h, :], acc[:, h, :], sqr[:, j % 2, :], ALU.add).then_inc(sq_added.sem, 1)

            v.memset(small[:, :], 0.0).then_inc(pre_vec, 1)
            v.memset(rows[:, :, :], 0.0).then_inc(pre_vec, 1)
            v.wait_ge(pre_vec, 2)
            v.memset(eps_c, EPS).then_inc(pre_vec, 1)
            v.memset(one_c, 1.0).then_inc(pre_vec, 1)
            v.sem_inc(emptied[0].sem, 1)
            v.sem_inc(emptied[1].sem, 1)
            v.sem_inc(emptied[2].sem, 1)
            v.sem_inc(emptied[3].sem, 1)
            for j in range(16):
                add_square(0, -16, j)
            v.wait_ge(const_landed, 32)
            norm_rows(0, -2, None)
            norm_apply(0, -16, -16, gain0, None)
            v.wait_ge(pos_landed, 16)
            n_pre = [4]

            def pre(ins):
                ins.then_inc(pre_vec, 1)
                n_pre[0] += 1
                v.wait_ge(pre_vec, n_pre[0])

            two_pi = 6.283185307179586
            c1 = 6.28125
            c2 = float(np.float32(np.round((two_pi - c1) * 2.0 ** 21) / 2.0 ** 21))
            c3 = float(np.float32(two_pi - c1 - c2))
            magic = 12582912.0
            pi_low = 3.1415925
            pre(v.tensor_copy(ang[:, 0, :], posi[:, :]))
            pre(v.tensor_scalar(ang[:, 0, :], ang[:, 0, :], const[:, C_FREQ:C_FREQ + 1], None, ALU.mult))
            for turn, (to, quarter_turn) in enumerate(((1, 0.0), (2, 0.25))):
                pre(v.tensor_scalar(ang[:, 3, :], ang[:, 0, :], 1.0 / two_pi, quarter_turn, ALU.mult, ALU.add))
                pre(v.tensor_scalar(ang[:, 3, :], ang[:, 3, :], magic, magic, ALU.add, ALU.subtract))
                pre(v.scalar_tensor_tensor(ang[:, to, :], ang[:, 3, :], -c1, ang[:, 0, :], ALU.mult, ALU.add))
                pre(v.scalar_tensor_tensor(ang[:, to, :], ang[:, 3, :], -c2, ang[:, to, :], ALU.mult, ALU.add))
                pre(v.scalar_tensor_tensor(ang[:, to, :], ang[:, 3, :], -c3, ang[:, to, :], ALU.mult, ALU.add))
                pre(v.tensor_scalar(ang[:, to, :], ang[:, to, :], quarter_turn * two_pi, pi_low, ALU.add, ALU.min))
                pre(v.tensor_scalar(ang[:, to, :], ang[:, to, :], -pi_low, None, ALU.max))
            assert n_pre[0] == PRE_VEC
            v.wait_ge(pre_act, 2)

            def conv(L, c):
                u = U_MQ + c
                if c == 0:
                    v.wait_ge(spilled, L * 16 + 16)
                v.wait_ge(emptied[bank(u, 0)].sem, emptied_at(L, u, 0))
                v.wait_ge(emptied[bank(u, 1)].sem, emptied_at(L, u, 1))
                r, dst = convraw[:, c % 2, :], qk[:, c, :]
                w = [par[:, A_CW + CONV * c + t:A_CW + CONV * c + t + 1] for t in range(CONV)]
                v.tensor_scalar(dst, r[:, 3:3 + S], w[3], par[:, A_CB + c:A_CB + c + 1], ALU.mult, ALU.add).then_inc(vec_step.sem, 1)
                v.wait_ge(vec_step.sem, step_at(L))
                for t in (2, 1, 0):
                    v.scalar_tensor_tensor(dst, r[:, t:t + S], w[t], dst, ALU.mult, ALU.add).then_inc(vec_step.sem, 1)
                    v.wait_ge(vec_step.sem, step_at(L, ("conv", c) if t == 0 else None))

            def running(L, src, bufs, op):
                for i in range(7):
                    sh, dst = 1 << i, bufs[i % 2]
                    a = src.rearrange("p (n c) -> p n c", c=CHUNK)
                    o = dst.rearrange("p (n c) -> p n c", c=CHUNK)
                    v.tensor_copy(o[:, :, 0:sh], a[:, :, 0:sh]).then_inc(vec_step.sem, 1)
                    count()
                    v.tensor_tensor(o[:, :, sh:], a[:, :, sh:], a[:, :, 0:CHUNK - sh], op).then_inc(vec_step.sem, 1)
                    v.wait_ge(vec_step.sem, step_at(L))
                    src = dst
                return src

            m_ = [mix[:, i, :] for i in range(5)]
            by_chunk = "p (n c) -> p n c"
            R4 = slice(0, MH)

            def gate_rows_1(L):
                v.wait_ge(emptied[bank(U_GATES, 0)].sem, emptied_at(L, U_GATES, 0))
                v.wait_ge(emptied[bank(U_GATES, 1)].sem, emptied_at(L, U_GATES, 1))
                v.tensor_scalar(m_[1][R4], m_[0][32:32 + MH], par[32:32 + MH, A_GB:A_GB + 1], None, ALU.add).then_inc(vec_step.sem, 1)
                v.wait_ge(vec_step.sem, step_at(L))
                v.scalar_tensor_tensor(m_[3][R4], m_[1][R4], -1.0, m_[1][R4], ALU.mult, ALU.min).then_inc(vec_step.sem, 1)
                v.wait_ge(vec_step.sem, step_at(L, "neg_abs"))

            def gate_rows_2(L):
                v.wait_ge(row_act.sem, row_act.at(L, 2))
                v.scalar_tensor_tensor(m_[2][R4], m_[1][R4], 0.0, m_[3][R4], ALU.min, ALU.subtract).then_inc(vec_step.sem, 1)
                v.wait_ge(vec_step.sem, step_at(L))
                running(L, m_[2][R4], [m_[3][R4], m_[4][R4]], ALU.add)

            def gate_rows_3(L):
                u, bc = rows[R4, 0, :], m_[3][R4]
                v.scalar_tensor_tensor(u, m_[0][R4], par[R4, A_GB:A_GB + 1], bc, ALU.add, ALU.subtract).then_inc(vec_step.sem, 1)
                v.wait_ge(vec_step.sem, step_at(L))
                running(L, u, [m_[4][R4], m_[2][R4]], ALU.max)

            def gate_rows_4(L):
                u, bc, cm = rows[R4, 0, :], m_[3][R4], m_[4][R4]
                bc3, cm3 = bc.rearrange(by_chunk, c=CHUNK), cm.rearrange(by_chunk, c=CHUNK)
                for n in range(NCH - 1):
                    v.scalar_tensor_tensor(mprev[:, n + 1:n + 2], mprev[:, n:n + 1], cm3[:, n, CHUNK - 1:],
                                           bc3[:, n, CHUNK - 1:], ALU.max, ALU.add).then_inc(vec_step.sem, 1)
                    v.wait_ge(vec_step.sem, step_at(L))
                mp = mprev.unsqueeze(2).to_broadcast([MH, NCH, CHUNK])
                big = m_[2][R4].rearrange(by_chunk, c=CHUNK)
                v.tensor_tensor(big, mp, cm3, ALU.max).then_inc(vec_step.sem, 1)
                v.wait_ge(vec_step.sem, step_at(L))
                v.tensor_scalar(rows[32:32 + MH, 0, :], m_[2][R4], -1.0, None, ALU.mult).then_inc(vec_step.sem, 1)
                v.wait_ge(vec_step.sem, step_at(L))
                v.tensor_tensor(m_[1][R4].rearrange(by_chunk, c=CHUNK), mp, big, ALU.subtract).then_inc(vec_step.sem, 1)
                v.wait_ge(vec_step.sem, step_at(L, "inter_log"))
                v.tensor_tensor(m_[4][R4], bc, m_[2][R4], ALU.add).then_inc(vec_step.sem, 1)
                v.wait_ge(vec_step.sem, step_at(L, "m_row"))
                v.tensor_tensor(m_[3][R4].rearrange(by_chunk, c=CHUNK), u.rearrange(by_chunk, c=CHUNK),
                                big[:, :, CHUNK - 1:].to_broadcast([MH, NCH, CHUNK]), ALU.subtract).then_inc(vec_step.sem, 1)
                v.wait_ge(vec_step.sem, step_at(L, "pw_log"))

            def gate_rows_5(L):
                v.wait_ge(row_act.sem, row_act.at(L, 3))
                v.tensor_scalar(rows[64:64 + MH, 0, :], m_[0][R4], MSCALE, None, ALU.mult).then_inc(vec_step.sem, 1)
                v.wait_ge(vec_step.sem, step_at(L))
                v.tensor_copy(rows[32:32 + MH, 1, 0:NCH],
                              m_[0][R4].rearrange(by_chunk, c=CHUNK)[:, :, CHUNK - 1]).then_inc(vec_step.sem, 1)
                v.wait_ge(vec_step.sem, step_at(L, "rows_end"))

            def key_blocks(L, n):
                if n >= 2:
                    v.wait_ge(aux_done.sem, aux_at(L, ("ms", n - 2)))
                for j in range(MC):
                    b = slice(2 * j, 2 * j + 2)
                    v.tensor_tensor(km[:, n % 2, b, :], qk[:, 3 + j:4 + j, P * n:P * n + P].to_broadcast([P, 2, P]),
                                    const[:, C_BLK + 2 * j:C_BLK + 2 * j + 2].unsqueeze(2).to_broadcast([P, 2, P]),
                                    ALU.mult).then_inc(vec_step.sem, 1)
                    count(("key_blocks", n))

            def ml_a(L, n):
                if n == 0:
                    v.wait_ge(silu_made.sem, silu_made.at(L, 6))
                    key_blocks(L, 0)
                    v.memset(kw[:, :, :], 0.0).then_inc(vec_step.sem, 1)
                    v.wait_ge(vec_step.sem, step_at(L))
                    v.memset(cst[:, 0, :, :], 0.0).then_inc(vec_step.sem, 1)
                    v.wait_ge(vec_step.sem, step_at(L, "c_zero"))
                    v.memset(vx[:, :, :, MD:MD + 1], 1.0).then_inc(vec_step.sem, 1)
                    v.wait_ge(vec_step.sem, step_at(L, "vx_ones"))
                    for b in range(4):
                        v.wait_ge(aux_read(("tt", b)), aux_read_at(L, ("tt", b)))
                    v.wait_ge(aux_read(("so",)), aux_read_at(L, ("so",)))
                v.wait_ge(aux_done.sem, aux_at(L, ("tk", n)))
                if n > 0:
                    v.wait_ge(aux_done.sem, aux_at(L, ("kv1", n - 1)))
                for b, (h, j, r0, r1) in enumerate(BLOCKS):
                    ins = v.tensor_scalar(kw[:, b, r0:r1], abank(("tk", n))[:, P * j + r0:P * j + r1],
                                          tt[:, n, 4, h:h + 1], None, ALU.mult)
                    if b < NB - 1:
                        ins.then_inc(vec_step.sem, 1)
                        count(("kw_first", n))
                    else:
                        ins.then_inc(aux_emptied[0].sem, 1)
                v.wait_ge(aux_done.sem, aux_at(L, ("mb", n)))
                mb = abank(("mb", n)).rearrange("p (h c) -> p h c", h=MH)
                if n < NCH - 1:
                    key_blocks(L, n + 1)
                for h in range(MH):
                    ins = v.scalar_tensor_tensor(dmat[:, h, :], mb[:, h, :], tt[:, n, 0, h:h + 1],
                                                 const[:, C_NEG:C_NEG + P], ALU.add, ALU.add)
                    if h < MH - 1:
                        ins.then_inc(vec_step.sem, 1)
                        count()
                    else:
                        ins.then_inc(aux_emptied[2].sem, 1)
                v.wait_ge(aux_done.sem, aux_at(L, ("ms", n)))
                v.wait_ge(d_exp.sem, d_exp.at(L, n + 1))
                v.scalar_tensor_tensor(smat.rearrange("p h c -> p (h c)"), abank(("ms", n)), MSCALE,
                                       dmat.rearrange("p h c -> p (h c)"), ALU.mult,
                                       ALU.mult).then_inc(aux_emptied[3].sem, 1)

            def ml_b(L, n):
                E = MD + 1
                v.wait_ge(aux_done.sem, aux_at(L, ("int", n)))
                v.tensor_tensor(tnum[:, :, :], abank(("int", n))[:, 0:MH * E].rearrange("p (h e) -> p h e", h=MH),
                                tt[:, n, 2, :].unsqueeze(2).to_broadcast([P, MH, E]),
                                ALU.mult).then_inc(aux_emptied[1].sem, 1)
                v.wait_ge(aux_read(("int", n)), aux_read_at(L, ("int", n)))
                v.tensor_tensor(num[:, :, :], abank(("num", n))[:, 0:MH * E].rearrange("p (h e) -> p h e", h=MH),
                                tnum[:, :, :], ALU.add).then_inc(aux_emptied[0].sem, 1)
                if n < NCH - 1:
                    a, b = cst[:, n % 2, :, :], cst[:, (n + 1) % 2, :, :]
                    if n > 0:
                        v.wait_ge(aux_read(("kv0", n - 1)), aux_read_at(L, ("kv0", n - 1)))
                        v.wait_ge(aux_read(("kv1", n - 1)), aux_read_at(L, ("kv1", n - 1)))
                    v.tensor_tensor(b, a, so6[:, :, n:n + 1].to_broadcast([P, NB, E]), ALU.mult).then_inc(vec_step.sem, 1)
                    v.wait_ge(vec_step.sem, step_at(L))
                    for i in range(2):
                        v.wait_ge(aux_done.sem, aux_at(L, (f"kv{i}", n)))
                        v.tensor_tensor(b[:, 3 * i:3 * i + 3, :], b[:, 3 * i:3 * i + 3, :],
                                        abank((f"kv{i}", n))[:, 0:3 * E].rearrange("p (b e) -> p b e", b=3),
                                        ALU.add).then_inc(aux_emptied[2 + i].sem, 1)
                v.wait_ge(aux_read(("num", n)), aux_read_at(L, ("num", n)))
                den3 = den_c.unsqueeze(2)
                v.scalar_tensor_tensor(den3, num[:, :, MD:E], -1.0, num[:, :, MD:E], ALU.mult, ALU.max).then_inc(vec_step.sem, 1)
                v.wait_ge(vec_step.sem, step_at(L))
                v.tensor_tensor(den_c, den_c, tt[:, n, 3, :], ALU.max).then_inc(vec_step.sem, 1)
                v.wait_ge(vec_step.sem, step_at(L))
                v.reciprocal(rden_c, den_c).then_inc(vec_step.sem, 1)
                v.wait_ge(vec_step.sem, step_at(L))
                hx = vm[:, n, :].rearrange("p (h d) -> p h d", h=MH)
                v.tensor_tensor(hx, num[:, :, 0:MD], rden_c.unsqueeze(2).to_broadcast([P, MH, MD]), ALU.mult).then_inc(vec_step.sem, 1)
                v.wait_ge(vec_step.sem, step_at(L))
                v.tensor_reduce(mean_c, hx, AX.X, ALU.add).then_inc(vec_step.sem, 1)
                v.wait_ge(vec_step.sem, step_at(L))
                v.tensor_scalar(mean_c, mean_c, -1.0 / MD, None, ALU.mult).then_inc(vec_step.sem, 1)
                v.wait_ge(vec_step.sem, step_at(L))
                v.tensor_tensor(hx, hx, mean_c.unsqueeze(2).to_broadcast([P, MH, MD]), ALU.add).then_inc(vec_step.sem, 1)
                v.wait_ge(vec_step.sem, step_at(L))
                v.tensor_tensor(tnum[:, :, 0:MD], hx, hx, ALU.mult).then_inc(vec_step.sem, 1)
                v.wait_ge(vec_step.sem, step_at(L))
                v.tensor_reduce(stat[:, 0, n, :], tnum[:, :, 0:MD], AX.X, ALU.add).then_inc(vec_step.sem, 1)
                v.wait_ge(vec_step.sem, step_at(L, ("ml_var", n)))

            def ml_fin(L):
                v.wait_ge(ml_rt.sem, ml_rt.at(L, 1))
                v.reciprocal(stat[:, 0, :, :], stat[:, 1, :, :]).then_inc(vec_step.sem, 1)
                v.wait_ge(vec_step.sem, step_at(L))
                for n in range(NCH):
                    hx = vm[:, n, :].rearrange("p (h d) -> p h d", h=MH)
                    v.tensor_tensor(hx, hx, stat[:, 0, n, :].unsqueeze(2).to_broadcast([P, MH, MD]),
                                    ALU.mult).then_inc(vec_step.sem, 1)
                    count(("ml_y", n))
                v.wait_ge(gated.sem, gated.at(L, 3))
                for j in range(MC):
                    for h in range(2):
                        name = ("yt", j, h)
                        v.wait_ge(aux_done.sem, aux_at(L, name))
                        o = mix[:, 5 + j, hs(h)]
                        v.scalar_tensor_tensor(o, abank(name), par[:, A_MG + j:A_MG + j + 1], o, ALU.mult,
                                               ALU.mult).then_inc(aux_read(name), 1)

            def shifted_add(L, dst, src, sh, r):
                v.tensor_copy(dst[r, 0:sh], src[r, 0:sh]).then_inc(vec_step.sem, 1)
                count()
                v.tensor_tensor(dst[r, sh:], src[r, sh:], src[r, 0:S - sh], ALU.add).then_inc(vec_step.sem, 1)
                v.wait_ge(vec_step.sem, step_at(L))

            def pool(L):
                every, low, high = slice(0, P), slice(0, 64), slice(64, P)
                for j in range(2):
                    v.wait_ge(emptied[bank(U_POOL + j, 0)].sem, emptied_at(L, U_POOL + j, 0))
                    v.wait_ge(emptied[bank(U_POOL + j, 1)].sem, emptied_at(L, U_POOL + j, 1))
                    u, a, b = mix[:, 3 + j, :], pool_t[:, 0, :], pool_t[:, 1, :]
                    shifted_add(L, a, u, 1, every)
                    if j == 0:
                        shifted_add(L, b, a, 2, high)
                        v.tensor_copy(b[low], a[low]).then_inc(vec_step.sem, 1)
                        v.wait_ge(vec_step.sem, step_at(L))
                        win = b
                    else:
                        shifted_add(L, b, a, 2, every)
                        shifted_add(L, a, b, 4, every)
                        shifted_add(L, b, a, 8, high)
                        v.tensor_copy(b[low], a[low]).then_inc(vec_step.sem, 1)
                        v.wait_ge(vec_step.sem, step_at(L))
                        win = b
                    v.tensor_tensor(tmp16[:, :], win[:, 0:16],
                                    const[:, C_INVC + 16 * j:C_INVC + 16 * j + 16], ALU.mult).then_inc(vec_step.sem, 1)
                    v.wait_ge(vec_step.sem, step_at(L))
                    v.tensor_tensor(tmp16[:, :], tmp16[:, :], u[:, 0:16], ALU.subtract).then_inc(vec_step.sem, 1)
                    v.wait_ge(vec_step.sem, step_at(L))
                    v.scalar_tensor_tensor(u, win, const[:, C_INVW + j:C_INVW + j + 1], u, ALU.mult,
                                           ALU.subtract).then_inc(vec_step.sem, 1)
                    v.wait_ge(vec_step.sem, step_at(L))
                    v.tensor_copy(u[:, 0:16], tmp16[:, :]).then_inc(vec_step.sem, 1)
                    v.wait_ge(vec_step.sem, step_at(L, ("pooled", j)))

            T0, QR, KR, QX, VT, KZ, SC0 = rw

            def rope(L, p):
                b = p % 2
                for which, (name, dst) in enumerate((("pq", QR), ("pk", KR))):
                    u = U_RET + 3 * p + which
                    v.wait_ge(emptied[bank(u, 0)].sem, emptied_at(L, u, 0))
                    v.wait_ge(emptied[bank(u, 1)].sem, emptied_at(L, u, 1))
                    v.tensor_tensor(T0[:, :], rqkv[:, b, which, :], cosT[:, :], ALU.mult).then_inc(vec_step.sem, 1)
                    v.wait_ge(vec_step.sem, step_at(L, ("cos_part", p, which)))
                    for h in range(2):
                        v.wait_ge(aux_done.sem, aux_at(L, (name, p, h)))
                        v.tensor_tensor(dst[:, hs(h)], abank((name, p, h)), sinT[:, hs(h)],
                                        ALU.mult).then_inc(aux_emptied[AUX[(name, p, h)][0]].sem, 1)
                    for h in range(2):
                        v.wait_ge(aux_read((name, p, h)), aux_read_at(L, (name, p, h)))
                        v.tensor_tensor(dst[:, hs(h)], dst[:, hs(h)], T0[:, hs(h)], ALU.add).then_inc(vec_step.sem, 1)
                        v.wait_ge(vec_step.sem, step_at(L, ("roped", p, which, h)))
                xi = const[:, C_XI + P * p:C_XI + P * p + P].unsqueeze(1).to_broadcast([P, NCH, P])
                v.tensor_tensor(QX.rearrange("p (n c) -> p n c", c=P), QR.rearrange("p (n c) -> p n c", c=P),
                                xi, ALU.mult).then_inc(vec_step.sem, 1)
                count(("q_xi", p))

            def turn(L, p):
                for h in range(2):
                    name = ("kz", p, h)
                    v.wait_ge(aux_done.sem, aux_at(L, name))
                    src = abank(name).rearrange("p (n e d) -> p n e d", n=4, e=2)
                    dst = KZ[:, hs(h)].rearrange("p (n e d) -> p n e d", n=4, e=2)
                    for e in range(2):
                        ins = v.tensor_scalar(dst[:, :, e, :], src[:, :, e, :],
                                              const[:, C_ZETA + 2 * p + e:C_ZETA + 2 * p + e + 1], None, ALU.mult)
                        if e == 0:
                            ins.then_inc(vec_step.sem, 1)
                            count(("kz_first", p, h))
                        else:
                            ins.then_inc(aux_read(name), 1)

            def scores(L, p):
                for e in range(2):
                    dst = SC0.rearrange("p (n c) -> p n c", c=P) if e == 0 else sc1[:, :, :]
                    dec = const[:, C_DEC + P * (2 * p + e):C_DEC + P * (2 * p + e) + P].unsqueeze(1).to_broadcast([P, 4, P])
                    for h in range(2):
                        name = ("rs", p, e, h)
                        v.wait_ge(aux_done.sem, aux_at(L, name))
                        v.tensor_tensor(dst[:, 4 * h:4 * h + 4, :], abank(name).rearrange("p (n c) -> p n c", c=P),
                                        dec, ALU.mult).then_inc(aux_read(name), 1)

            def state(L, p):
                v.memset(rst[:, 0, :], 0.0).then_inc(vec_step.sem, 1)
                v.wait_ge(vec_step.sem, step_at(L))
                v.wait_ge(aux_done.sem, aux_at(L, ("rkv", p)))
                kvp = abank(("rkv", p)).rearrange("p (n d) -> p n d", n=NCH)
                for n in range(NCH - 1):
                    ins = v.scalar_tensor_tensor(rst[:, n + 1, :], rst[:, n, :], const[:, C_GAM + p:C_GAM + p + 1],
                                                 kvp[:, n, :], ALU.mult, ALU.add)
                    if n < NCH - 2:
                        ins.then_inc(vec_step.sem, 1)
                        v.wait_ge(vec_step.sem, step_at(L))
                    else:
                        ins.then_inc(aux_emptied[0].sem, 1)

            def spread(L, p):
                for h in range(2):
                    v.wait_ge(aux_read(("rv", p, h)), aux_read_at(L, ("rv", p, h)))
                    v.reciprocal(KZ[:, hs(h)], KZ[:, hs(h)]).then_inc(vec_step.sem, 1)
                    v.wait_ge(vec_step.sem, step_at(L))
                    v.scalar_tensor_tensor(KR[:, hs(h)], KR[:, hs(h)], par[:, A_RG + p:A_RG + p + 1],
                                           KZ[:, hs(h)], ALU.mult, ALU.mult).then_inc(vec_step.sem, 1)
                    v.wait_ge(vec_step.sem, step_at(L))
                    v.wait_ge(gated.sem, gated.at(L, 4 + p))
                    v.tensor_tensor(mix[:, p, hs(h)], mix[:, p, hs(h)], KR[:, hs(h)], ALU.mult).then_inc(vec_step.sem, 1)
                    v.wait_ge(vec_step.sem, step_at(L, ("ret_mix", p, h)))

            def mix_split(L):
                for i in range(16):
                    h, c = i // 8, MIX_ORDER[i % 8]
                    v.wait_ge(h_hi.sem, h_hi.at(L, i + 1))
                    v.tensor_tensor(hl[:, c, hs(h)], mix[:, c, hs(h)], hh[:, c, hs(h)].bitcast(F32),
                                    ALU.subtract).then_inc(h_ready.sem, 1)

            def add_fill(L, u, k, m, h, more=0, more_units=0, told=0):
                v.wait_ge(filled(u, k), filled_at(L, u, k, told, more_units))
                v.tensor_tensor(x[:, m, hs(h)], x[:, m, hs(h)], pbank(u, k),
                                ALU.add).then_inc(emptied[bank(u, k)].sem, 1)

            def norm(L, i):
                norm_rows(L, 2 * i, i)
                norm_apply(L, 16 * i, 16 * (i + 1), par[:, 8 * i:8 * i + 8], i)

            def ffn_up(L, u, g, lp):
                for f in range(2):
                    for h in range(2):
                        ug, uu = u + 2 * f, u + 2 * f + 1
                        v.wait_ge(emptied[bank(ug, h)].sem, emptied_at(L, ug, h, lp.fills))
                        v.wait_ge(filled(uu, h), filled_at(L, uu, h, lp.told, lp.units))
                        if not (type(lp.acts) is int and g == 0 and f == 0):
                            v.wait_ge(act_ready.sem, act_ready.at(L, lp.acts + (4 * g + 2 * f - 1 + h)))
                        v.tensor_tensor(act_t[:, h, :], silu_g[:, h, :], pbank(uu, h),
                                        ALU.mult).then_inc(emptied[bank(uu, h)].sem, 1)
                    for h in range(2):
                        v.wait_ge(act_hi_made.sem, act_hi_made.at(L, lp.acts + (4 * g + 2 * f + h + 1)))
                        v.wait_ge(emptied[bank(u + 2 * f + 1, h)].sem, emptied_at(L, u + 2 * f + 1, h, lp.fills))
                        v.tensor_tensor(alo[:, g % 2, f, hs(h)], act_t[:, h, :], ahi[:, g % 2, f, hs(h)].bitcast(F32),
                                        ALU.subtract).then_inc(act_ready.sem, 1)

            def ffn_down(L, u, lp, last):
                for k in range(16):
                    uu, kk = u + k // 8, k % 8
                    add_fill(L, uu, kk, k // 2, k % 2, 0, lp.units, lp.told)
                    if last and k >= 1:
                        add_square(L, 16, k - 1)
                if last:
                    add_square(L, 16, 15)

            with v.Fori(0, DEPTH) as L:
                v.wait_ge(par_landed, L * 16 + 16)
                steps[0] = 0
                v.memset(convraw[:, :, 0:CONV - 1], 0.0).then_inc(vec_step.sem, 1)
                v.wait_ge(vec_step.sem, step_at(L, "pads"))
                for item in MACRO:
                    what, args = item[0], item[1:]
                    if what == "unit" and U_MQ <= args[0] < U_MV:
                        if args[0] == U_MQ:
                            gate_rows_1(L)
                        conv(L, args[0] - U_MQ)
                        if args[0] == U_MQ + 1:
                            gate_rows_2(L)
                        elif args[0] == U_MQ + 3:
                            gate_rows_3(L)
                        elif args[0] == U_MQ + 5:
                            gate_rows_4(L)
                            gate_rows_5(L)
                    elif what == "ml_a":
                        ml_a(L, *args)
                    elif what == "ml_b":
                        ml_b(L, *args)
                    elif what == "ml_fin":
                        ml_fin(L)
                    elif what == "pool":
                        pool(L)
                    elif what == "rope":
                        rope(L, *args)
                    elif what == "turn":
                        turn(L, *args)
                    elif what == "scores":
                        scores(L, *args)
                    elif what == "state":
                        state(L, *args)
                    elif what == "spread":
                        spread(L, *args)
                    elif what == "mix_split":
                        mix_split(L)
                    elif what == "out_units":
                        v.wait_ge(reloaded, L * 16 + 16)
                        for j in range(16):
                            add_fill(L, U_OUT + j // 2, j % 2, j // 2, j % 2)
                            if j >= 1:
                                add_square(L, 0, j - 1)
                        add_square(L, 0, 15)
                    elif what == "norm":
                        norm(L, *args)
                    elif what == "p_split":
                        for k in range(2):
                            v.wait_ge(p_hi_made.sem, p_hi_made.at(L, k + 1))
                            v.tensor_tensor(plo[:, k, :], praw[:, k, :], phi[:, k, :].bitcast(F32),
                                            ALU.subtract).then_inc(p_ready.sem, 1)
                    elif what == "ffn":
                        ffn_up(L, U_FFN, 0, LoopValues(0))
                        with v.Fori(0, FG // 2) as i:
                            lp = LoopValues(i)
                            ffn_up(L, U_FFN + 4, 1, lp)
                            ffn_down(L, U_FFN + 8, lp, False)
                            ffn_up(L, U_FFN + 10, 2, lp)
                            ffn_down(L, U_FFN + 14, lp, False)
                        ffn_down(L, U_PROJ - 2, LoopValues(0), True)
                    elif what == "ple_proj":
                        norm(L, 1)
                    elif what == "ple_gate":
                        for j in range(16):
                            m, h = divmod(j, 2)
                            v.wait_ge(emptied[bank(U_GATE + m, h)].sem, emptied_at(L, U_GATE + m, h))
                            v.tensor_tensor(pt[:, h, :], psg[:, h, :], pp[:, m, hs(h)], ALU.mult).then_inc(vec_step.sem, 1)
                            v.wait_ge(vec_step.sem, step_at(L, ("ple_t", j)))
                            v.tensor_tensor(x[:, m, hs(h)], x[:, m, hs(h)], pt[:, h, :],
                                            ALU.add).then_inc(x_ple.sem, 1)
                            v.wait_ge(x_ple.sem, x_ple.at(L, j + 1))
                            if j >= 1:
                                add_square(L, 32, j - 1)
                        add_square(L, 32, 15)
                assert steps[0] == VEC_STEPS, steps[0]
            for j in range(16):
                h, c = divmod(j, 8)
                v.wait_ge(h_ready.sem, h_ready.at(DEPTH, -16 + j + 1))
                v.wait_ge(h_hi.sem, h_hi.at(DEPTH, -16 + j + 1))
                v.tensor_tensor(x[:, c, hs(h)], hh[:, c, hs(h)].bitcast(F32), hl[:, c, hs(h)].bitcast(F32),
                                ALU.add).then_inc(result, 1)

        @block.scalar
        def _(a):
            def square(L, base, j, final):
                c, h = divmod(j, 2)
                final(c, h, j)
                if not (type(L) is int and base + j + 16 < 2):
                    a.wait_ge(sq_added.sem, sq_added.at(L, base + j - 1))
                a.activation(sqr[:, j % 2, :], x[:, c, hs(h)], ACT.Square).then_inc(sq_made.sem, 1)

            def roots(L, i):
                for h in range(2):
                    if i is None:
                        a.wait_ge(aux_done.sem, h + 1)
                    else:
                        a.wait_ge(aux_done.sem, aux_at(L, ("sum", i, h)))
                    a.activation(rt_c[:, 4 * h:4 * h + 4], aux[:, h, 0:4], ACT.Sqrt, bias=eps_c,
                                 scale=1.0 / D).then_inc(aux_emptied[h].sem, 1)

            def rows_out(L, i):
                for h in range(2):
                    if i is None:
                        a.wait_ge(aux_done.sem, h + 3)
                    else:
                        a.wait_ge(aux_done.sem, aux_at(L, ("row", i, h)))
                    a.activation(rstd[:, h, :], aux[:, 2 + h, :], ACT.Copy).then_inc(aux_emptied[2 + h].sem, 1)

            def highs(L, base, hbase):
                for j in range(16):
                    h, c = divmod(j, 8)
                    a.wait_ge(normed.sem, normed.at(L, base + j + 1))
                    a.activation(hh[:, c, hs(h)], nt[:, j % 2, :], ACT.Copy).then_inc(h_hi.sem, 1)

            a.dma_start(x[:, :, :], x_d).then_inc(x_landed, 16)
            a.dma_start(const[:, :], const_d).then_inc(const_landed, 16)
            a.dma_start(gain0[:, :], gain0_d).then_inc(const_landed, 16)
            a.dma_start(posi[:, :], pos_d.partition_broadcast(P)).then_inc(pos_landed, 16)
            a.wait_ge(pre_vec, 4)
            a.wait_ge(x_landed, 16)
            for j in range(16):
                square(0, -16, j, lambda c, h, j: None)
            roots(0, None)
            rows_out(0, None)
            highs(0, -16, -16)
            a.wait_ge(pre_vec, PRE_VEC)
            a.activation(sinT[:, :], ang[:, 1, :], ACT.Sin).then_inc(pre_act, 1)
            a.activation(cosT[:, :], ang[:, 2, :], ACT.Sin).then_inc(pre_act, 1)

            def evacuate(L, u, k):
                if U_MQ <= u < U_MV and k == 0:
                    c = u - U_MQ
                    if c == 0:
                        a.wait_ge(vec_step.sem, mark_at(L, "pads"))
                    if c >= 2:
                        a.wait_ge(vec_step.sem, mark_at(L, ("conv", c - 2)))
                if u == U_RG and k == 0:
                    a.wait_ge(vec_step.sem, mark_at(L, "rows_end"))
                if u >= U_RET + 6 and k == 0:
                    w = (u - U_RET) % 3
                    if w < 2:
                        a.wait_ge(vec_step.sem, mark_at(L, ("cos_part", 0, w)))
                a.wait_ge(filled(u, k), filled_at(L, u, k))
                src, sl = pbank(u, k), hs(k)
                if u == U_GATES:
                    src, dst = src[0:64], mix[0:64, 0, sl]
                elif u < U_MV:
                    dst = convraw[:, (u - U_MQ) % 2, CONV - 1 + HALF * k:CONV - 1 + HALF * k + HALF]
                elif u < U_MO:
                    j = u - U_MV
                    dst = vm[:, 4 * k:4 * k + 4, P * j:P * j + P]
                    src = src.rearrange("p (n c) -> p n c", c=P)
                elif u < U_RG:
                    dst = mix[:, 5 + u - U_MO, sl]
                elif u < U_POOL:
                    dst = mix[:, u - U_RG, sl]
                elif u < U_RET:
                    dst = mix[:, 3 + u - U_POOL, sl]
                else:
                    p, w = divmod(u - U_RET, 3)
                    dst = rqkv[:, p % 2, w, sl]
                a.activation(dst, src, ACT.Copy).then_inc(emptied[bank(u, k)].sem, 1)

            T0, QR, KR, QX, VT, KZ, SC0 = rw
            by = "p (n c) -> p n c"

            with a.Fori(0, DEPTH) as L:
                a.wait_ge(h_ready.sem, h_ready.at(L, 0))
                a.dma_start(par[:, :], par_d[L]).then_inc(par_landed, 16)
                a.dma_start(spill_d, x[:, :, :]).then_inc(spilled, 16)
                for item in MACRO:
                    what, args = item[0], item[1:]
                    if what == "unit":
                        u = args[0]
                        for k in range(2):
                            evacuate(L, u, k)
                        if u == U_MQ + 1:
                            a.wait_ge(vec_step.sem, mark_at(L, "neg_abs"))
                            a.activation(mix[0:MH, 3, :], mix[0:MH, 3, :], ACT.Exp).then_inc(row_act.sem, 1)
                            a.wait_ge(row_act.sem, row_act.at(L, 1))
                            a.activation(mix[0:MH, 3, :], mix[0:MH, 3, :], ACT.Ln,
                                         bias=one_c[0:MH]).then_inc(row_act.sem, 1)
                        if u == U_MV + 1:
                            a.wait_ge(vec_step.sem, mark_at(L, "inter_log"))
                            a.activation(mix[0:MH, 0, :], mix[0:MH, 1, :], ACT.Exp).then_inc(row_act.sem, 1)
                            a.wait_ge(vec_step.sem, mark_at(L, "m_row"))
                            a.activation(rows[96:96 + MH, 0, :], mix[0:MH, 4, :], ACT.Exp,
                                         scale=-1.0).then_inc(row_act.sem, 1)
                            a.wait_ge(vec_step.sem, mark_at(L, "pw_log"))
                            a.activation(rows[0:MH, 1, :], mix[0:MH, 3, :], ACT.Exp).then_inc(row_act.sem, 1)
                        if u == U_MV + 2:
                            for c in range(6):
                                a.wait_ge(vec_step.sem, mark_at(L, ("conv", c)))
                                a.activation(qk[:, c, :], qk[:, c, :], ACT.Silu).then_inc(silu_made.sem, 1)
                    elif what == "half":
                        evacuate(L, *args)
                    elif what == "ml_cols":
                        for b in range(4):
                            a.wait_ge(aux_done.sem, aux_at(L, ("tt", b)))
                            src = abank(("tt", b)).rearrange("p (n q h) -> p n q h", n=2, q=8)
                            a.activation(tt[:, 2 * b:2 * b + 2, :, :], src[:, :, 0:5, 0:MH],
                                         ACT.Copy).then_inc(aux_emptied[b].sem, 1)
                        a.wait_ge(aux_done.sem, aux_at(L, ("so",)))
                        a.activation(so6.rearrange("p b n -> p (b n)"), abank(("so",))[:, 0:NB * NCH],
                                     ACT.Copy).then_inc(aux_emptied[0].sem, 1)
                    elif what == "ml_a":
                        n = args[0]
                        a.wait_ge(aux_done.sem, aux_at(L, ("tv", n)))
                        if n == 0:
                            a.wait_ge(vec_step.sem, mark_at(L, "vx_ones"))
                        a.activation(vx[:, n % 2, :, 0:MD], abank(("tv", n))[:, 0:MW].rearrange("p (h d) -> p h d", h=MH),
                                     ACT.Copy).then_inc(aux_emptied[1].sem, 1)
                        a.wait_ge(aux_read(("mb", n)), aux_read_at(L, ("mb", n)))
                        a.activation(dmat.rearrange("p h c -> p (h c)"), dmat.rearrange("p h c -> p (h c)"),
                                     ACT.Exp).then_inc(d_exp.sem, 1)
                    elif what == "gate_funcs":
                        for i, c in enumerate((5, 6, 7, 0, 1, 2)):
                            u = U_MO + i
                            a.wait_ge(emptied[bank(u, 0)].sem, emptied_at(L, u, 0))
                            a.wait_ge(emptied[bank(u, 1)].sem, emptied_at(L, u, 1))
                            a.activation(mix[:, c, :], mix[:, c, :], ACT.Sigmoid if i < 3 else ACT.Silu).then_inc(gated.sem, 1)
                        a.wait_ge(vec_step.sem, mark_at(L, ("ml_var", NCH - 1)))
                        a.activation(stat[:, 1, :, :], stat[:, 0, :, :], ACT.Sqrt, bias=eps_c,
                                     scale=1.0 / MD).then_inc(ml_rt.sem, 1)
                    elif what == "pool":
                        for j in range(2):
                            for h in range(2):
                                name = ("pm", j, h)
                                a.wait_ge(aux_done.sem, aux_at(L, name))
                                a.activation(mix[:, 3 + j, hs(h)], abank(name), ACT.Copy,
                                             scale=par[:, A_PS + j:A_PS + j + 1]).then_inc(aux_read(name), 1)
                    elif what == "turn":
                        p = args[0]
                        for h in range(2):
                            name = ("vt", p, h)
                            a.wait_ge(aux_done.sem, aux_at(L, name))
                            a.activation(VT[:, hs(h)], abank(name), ACT.Copy).then_inc(aux_read(name), 1)
                    elif what == "ret_y":
                        p = args[0]
                        for h in range(2):
                            name = ("ry", p, h)
                            a.wait_ge(aux_done.sem, aux_at(L, name))
                            a.activation(T0[:, hs(h)], abank(name), ACT.Copy).then_inc(aux_read(name), 1)
                    elif what == "centre":
                        p = args[0]
                        for h in range(2):
                            name = ("rc", p, h)
                            a.wait_ge(aux_done.sem, aux_at(L, name))
                            a.activation(KR[:, hs(h)], abank(name), ACT.Copy).then_inc(aux_read(name), 1)
                            a.wait_ge(aux_read(name), aux_read_at(L, name))
                            a.activation(QX[:, hs(h)], KR[:, hs(h)], ACT.Square).then_inc(ret_sq.sem, 1)
                    elif what == "spread":
                        p = args[0]
                        for h in range(2):
                            name = ("rv", p, h)
                            a.wait_ge(aux_done.sem, aux_at(L, name))
                            a.activation(KZ[:, hs(h)], abank(name), ACT.Sqrt,
                                         bias=eps_c).then_inc(aux_read(name), 1)
                    elif what == "mix_split":
                        a.wait_ge(unit_done.sem, unit_done.at(L, U_OUT))
                        for i in range(16):
                            h, c = i // 8, MIX_ORDER[i % 8]
                            if c < 3:
                                a.wait_ge(vec_step.sem, mark_at(L, ("ret_mix", c, h)))
                            elif c < 5:
                                a.wait_ge(aux_read(("pm", c - 3, h)), aux_read_at(L, ("pm", c - 3, h)))
                            else:
                                a.wait_ge(aux_read(("yt", c - 5, h)), aux_read_at(L, ("yt", c - 5, h)))
                            a.activation(hh[:, c, hs(h)], mix[:, c, hs(h)], ACT.Copy).then_inc(h_hi.sem, 1)
                            if i == 15:
                                a.dma_start(x[:, :, :], spill_d).then_inc(reloaded, 16)
                                a.dma_start(praw[:, :, :], p_d[L]).then_inc(p_landed, 16)
                    elif what == "out_units":
                        for j in range(16):
                            square(L, 0, j, lambda c, h, j: a.wait_ge(emptied[bank(U_OUT + c, h)].sem, emptied_at(L, U_OUT + c, h)))
                    elif what == "norm":
                        i = args[0]
                        roots(L, i)
                        rows_out(L, i)
                        highs(L, 16 * i, 16 * (i + 1))
                    elif what == "p_split":
                        a.wait_ge(p_landed, L * 16 + 16)
                        for k in range(2):
                            a.activation(phi[:, k, :], praw[:, k, :], ACT.Copy).then_inc(p_hi_made.sem, 1)
                    elif what == "ffn":
                        def ffn_up(u, g, lp):
                            for f in range(2):
                                ug, uu = u + 2 * f, u + 2 * f + 1
                                for h in range(2):
                                    a.wait_ge(filled(ug, h), filled_at(L, ug, h, lp.told, lp.units))
                                    if not (type(lp.acts) is int and g == 0 and f == 0):
                                        a.wait_ge(act_ready.sem, act_ready.at(L, lp.acts + (4 * g + 2 * f - 1 + h)))
                                    elif h == 0:
                                        a.wait_ge(h_ready.sem, h_ready.at(L, 32))
                                    a.activation(silu_g[:, h, :], pbank(ug, h),
                                                 ACT.Silu).then_inc(emptied[bank(ug, h)].sem, 1)
                                for h in range(2):
                                    a.wait_ge(emptied[bank(uu, h)].sem, emptied_at(L, uu, h, lp.fills))
                                    a.activation(ahi[:, g % 2, f, hs(h)], act_t[:, h, :],
                                                 ACT.Copy).then_inc(act_hi_made.sem, 1)

                        ffn_up(U_FFN, 0, LoopValues(0))
                        with a.Fori(0, FG // 2) as i:
                            lp = LoopValues(i)
                            ffn_up(U_FFN + 4, 1, lp)
                            ffn_up(U_FFN + 10, 2, lp)
                        for j in range(16):
                            square(L, 16, j, lambda c, h, j: a.wait_ge(emptied[bank(U_PROJ - 2 + j // 8, j % 8)].sem, emptied_at(L, U_PROJ - 2 + j // 8, j % 8)))
                    elif what == "ple_proj":
                        def out(k):
                            u, kk = U_PROJ + k // 8, k % 8
                            a.wait_ge(filled(u, kk), filled_at(L, u, kk))
                            a.activation(pp[:, k // 2, hs(k % 2)], pbank(u, kk),
                                         ACT.Copy).then_inc(emptied[bank(u, kk)].sem, 1)
                        for k in range(8):
                            out(k)
                        roots(L, 1)
                        for k in range(8, 12):
                            out(k)
                        rows_out(L, 1)
                        for k in range(12, 16):
                            out(k)
                        highs(L, 16, 32)
                    elif what == "ple_gate":
                        for j in range(17):
                            if j < 16:
                                m, h = divmod(j, 2)
                                a.wait_ge(filled(U_GATE + m, h), filled_at(L, U_GATE + m, h))
                                if j >= 2:
                                    a.wait_ge(vec_step.sem, mark_at(L, ("ple_t", j - 2)))
                                a.activation(psg[:, h, :], pbank(U_GATE + m, h),
                                             ACT.Sigmoid).then_inc(emptied[bank(U_GATE + m, h)].sem, 1)
                            if j >= 1:
                                square(L, 32, j - 1, lambda c, h, jj: a.wait_ge(x_ple.sem, x_ple.at(L, jj + 1)))
            for h in range(2):
                a.wait_ge(result, 8 * h + 8)
                a.dma_start(out_d[:, :, hs(h)], x[:, :, hs(h)]).then_inc(out_stored, 16)
            a.wait_ge(out_stored, 32)

        @block.sync
        def _(sp):
            with sp.Fori(0, DEPTH * UNITS // RING) as i:
                for r in range(RING):
                    sp.wait_ge(weights_ready.sem, i * RING + (r + 1))
                    sp.dma_start(raw[:, r, :], w_d[i * RING + r]).then_inc(raw_landed[r], 16)

        @block.gpsimd
        def _(g):
            g.memset(zero1[:, :], 0.0).then_inc(w_hi_made, 1)
            g.sem_inc(weights_ready.sem, RING)
            g.wait_ge(w_hi_made, 1)
            with g.Fori(0, DEPTH * UNITS // RING) as i:
                for r in range(RING):
                    g.wait_ge(unit_done.sem, i * RING + (r + 1))
                    g.wait_ge(raw_landed[r], i * 16 + 16)
                    g.tensor_tensor(whi[:, r, :], raw[:, r, :], zero1[:, 0:1].to_broadcast([P, 1024]),
                                    ALU.add).then_inc(w_hi_made, 1)
                    g.wait_ge(w_hi_made, i * RING + (r + 2))
                    g.tensor_tensor(wlo[:, r, :], raw[:, r, :], whi[:, r, :].bitcast(F32),
                                    ALU.subtract).then_inc(weights_ready.sem, 1)

        @block.tensor
        def _(pe):
            pe.sem_inc(unit_done.sem, RING)
            T0, QR, KR, QX, VT, KZ, SC0 = rw

            def product(out, u, slot_w, col, ks, rhi, rlo, ready=None):
                last = None
                for i, (k, wk) in enumerate(ks):
                    if ready is not None:
                        ready(i, k)
                    wh, wl = whi[:, slot_w, wk + col:wk + col + P], wlo[:, slot_w, wk + col:wk + col + P]
                    pe.matmul(out, wh, rhi(k), start=(i == 0), stop=False)
                    pe.matmul(out, wl, rhi(k), start=False, stop=False)
                    last = pe.matmul(out, wh, rlo(k), start=False, stop=(i == len(ks) - 1))
                return last

            def tell(ins, u, k):
                ins.then_inc(unit_done.sem if k == unit_fills(u) - 1 else fill_done.sem, 1)

            def narrow(L, u, h, order=range(KC), ready=None, fills=0, units=0):
                if h == 0:
                    pe.wait_ge(weights_ready.sem, weights_ready.at(L, units + (u + 1)))
                pe.wait_ge(emptied[bank(u, h)].sem, free_at(L, u, h, fills))
                tell(product(pbank(u, h), u, u % RING, 0, [(k, P * k) for k in order],
                             lambda k: hh[:, k, hs(h)], lambda k: hl[:, k, hs(h)], ready), u, h)

            def wide(L, u, k, rhi, rlo, fills=0, units=0):
                if k == 0:
                    pe.wait_ge(weights_ready.sem, weights_ready.at(L, units + (u + 1)))
                pe.wait_ge(emptied[bank(u, k)].sem, free_at(L, u, k, fills))
                m, h = divmod(k, 2)
                tell(product(pbank(u, k), u, u % RING, P * m, [(0, 0), (1, HALF)],
                             lambda c: rhi[:, c, hs(h)], lambda c: rlo[:, c, hs(h)]), u, k)

            def free(L, name):
                b, _, i = AUX[name]
                aux_emptied[b].wait(pe, L, i)

            def sums(L, base, i):
                for h in range(2):
                    pe.wait_ge(sq_added.sem, sq_added.at(L, base + 15 + h))
                    if i is not None:
                        pe.wait_ge(aux_read(("sum", i, h)), aux_free_at(L, ("sum", i, h)))
                    for t in range(4):
                        ins = pe.matmul(aux[:, h, t:t + 1], acc[:, h, P * t:P * t + P], ones[:, 0:1],
                                        start=True, stop=True)
                    ins.then_inc(aux_done.sem, 1)

            def spread_rstd(L, dbase, i):
                for h in range(2):
                    pe.wait_ge(diag_made.sem, diag_made.at(L, dbase + h + 1))
                    if i is not None:
                        pe.wait_ge(aux_read(("row", i, h)), aux_free_at(L, ("row", i, h)))
                    pe.matmul(aux[:, 2 + h, :], ones, diag.rearrange("p t c -> p (t c)"),
                                       start=True, stop=True).then_inc(aux_done.sem, 1)

            pe.wait_ge(const_landed, 32)
            sums(0, -16, None)
            spread_rstd(0, -2, None)

            with pe.Fori(0, DEPTH) as L:
                for item in MACRO:
                    what, args = item[0], item[1:]
                    if what == "unit":
                        u = args[0]
                        for h in range(2):
                            ready = None
                            if u == U_GATES:
                                ready = lambda i, k, h=h: pe.wait_ge(h_ready.sem, h_ready.at(L, -16 + 8 * h + k + 1))
                            narrow(L, u, h, ready=ready)
                    elif what == "half":
                        narrow(L, *args)
                    elif what == "ml_cols":
                        pe.wait_ge(vec_step.sem, mark_at(L, "rows_end"))
                        pe.wait_ge(row_act.sem, row_act.at(L, 5))
                        for b in range(4):
                            pe.wait_ge(aux_read(("tt", b)), aux_free_at(L, ("tt", b)))
                            for n in (2 * b, 2 * b + 1):
                                for s in range(2):
                                    o = (n % 2) * 256 + s * P
                                    ins = pe.transpose(abank(("tt", b))[:, o:o + P], rows[:, s, P * n:P * n + P], ident)
                            ins.then_inc(aux_done.sem, 1)
                        pe.wait_ge(aux_read(("so",)), aux_free_at(L, ("so",)))
                        for i, (h, *_) in enumerate(BLOCKS):
                            ins = pe.matmul(abank(("so",))[:, NCH * i:NCH * i + NCH],
                                            const[32:32 + MH, C_SEL + P * h:C_SEL + P * h + P],
                                            rows[32:32 + MH, 1, 0:NCH], start=True, stop=True)
                        ins.then_inc(aux_done.sem, 1)
                    elif what == "ml_a":
                        n = args[0]
                        cs = slice(P * n, P * n + P)
                        if n == 0:
                            pe.wait_ge(silu_made.sem, silu_made.at(L, 6))
                            for u in range(U_MV, U_MO):
                                pe.wait_ge(emptied[bank(u, 0)].sem, emptied_at(L, u, 0))
                                pe.wait_ge(emptied[bank(u, 1)].sem, emptied_at(L, u, 1))
                        pe.wait_ge(aux_read(("tk", n)), aux_free_at(L, ("tk", n)))
                        for j in range(MC):
                            ins = pe.transpose(abank(("tk", n))[:, P * j:P * j + P], qk[:, 3 + j, cs], ident)
                        ins.then_inc(aux_done.sem, 1)
                        pe.wait_ge(aux_read(("tv", n)), aux_free_at(L, ("tv", n)))
                        for j in range(MC):
                            ins = pe.transpose(abank(("tv", n))[:, P * j:P * j + P], vm[:, n, P * j:P * j + P], ident)
                        ins.then_inc(aux_done.sem, 1)
                        pe.wait_ge(aux_read(("mb", n)), aux_free_at(L, ("mb", n)))
                        for h in range(MH):
                            ins = pe.matmul(abank(("mb", n))[:, P * h:P * h + P],
                                            const[32:32 + MH, C_SEL + P * h:C_SEL + P * h + P],
                                            rows[32:32 + MH, 0, cs], start=True, stop=True)
                        ins.then_inc(aux_done.sem, 1)
                        pe.wait_ge(aux_read(("ms", n)), aux_free_at(L, ("ms", n)))
                        pe.wait_ge(vec_step.sem, mark_at(L, ("key_blocks", n)))
                        for b, (h, j, *_) in enumerate(BLOCKS):
                            ins = pe.matmul(abank(("ms", n))[:, P * h:P * h + P], km[:, n % 2, b, :], qk[:, j, cs],
                                            start=b == 0 or BLOCKS[b - 1][0] != h,
                                            stop=b == NB - 1 or BLOCKS[b + 1][0] != h)
                        ins.then_inc(aux_done.sem, 1)
                    elif what == "ml_b":
                        n = args[0]
                        cs, E = slice(P * n, P * n + P), MD + 1
                        pe.wait_ge(aux_read(("ms", n)), aux_read_at(L, ("ms", n)))
                        pe.wait_ge(aux_read(("tv", n)), aux_read_at(L, ("tv", n)))
                        pe.wait_ge(aux_read(("num", n)), aux_free_at(L, ("num", n)))
                        for h in range(MH):
                            ins = pe.matmul(abank(("num", n))[:, E * h:E * h + E], smat[:, h, :], vx[:, n % 2, h, :],
                                            start=True, stop=True)
                        ins.then_inc(aux_done.sem, 1)
                        if n > 0:
                            pe.wait_ge(aux_read(("kv0", n - 1)), aux_read_at(L, ("kv0", n - 1)))
                            pe.wait_ge(aux_read(("kv1", n - 1)), aux_read_at(L, ("kv1", n - 1)))
                        else:
                            pe.wait_ge(vec_step.sem, mark_at(L, "c_zero"))
                        pe.wait_ge(aux_read(("int", n)), aux_free_at(L, ("int", n)))
                        for b, (h, j, *_) in enumerate(BLOCKS):
                            ins = pe.matmul(abank(("int", n))[:, E * h:E * h + E], qk[:, j, cs], cst[:, n % 2, b, :],
                                            start=b == 0 or BLOCKS[b - 1][0] != h,
                                            stop=b == NB - 1 or BLOCKS[b + 1][0] != h)
                        ins.then_inc(aux_done.sem, 1)
                        if n < NCH - 1:
                            pe.wait_ge(vec_step.sem, mark_at(L, ("kw_first", n)))
                            pe.wait_ge(aux_read(("tk", n)), aux_read_at(L, ("tk", n)))
                            for i in range(2):
                                pe.wait_ge(aux_read((f"kv{i}", n)), aux_free_at(L, (f"kv{i}", n)))
                                for b in range(3):
                                    h = BLOCKS[3 * i + b][0]
                                    ins = pe.matmul(abank((f"kv{i}", n))[:, E * b:E * b + E], kw[:, 3 * i + b, :],
                                                    vx[:, n % 2, h, :], start=True, stop=True)
                                ins.then_inc(aux_done.sem, 1)
                    elif what == "ml_fin":
                        for j in range(MC):
                            for h in range(2):
                                name = ("yt", j, h)
                                pe.wait_ge(vec_step.sem, mark_at(L, ("ml_y", 4 * h + 3)))
                                pe.wait_ge(aux_read(name), aux_free_at(L, name))
                                for n in range(4):
                                    ins = pe.transpose(abank(name)[:, P * n:P * n + P], vm[:, 4 * h + n, P * j:P * j + P], ident)
                                ins.then_inc(aux_done.sem, 1)
                    elif what == "pool":
                        for j in range(2):
                            pe.wait_ge(vec_step.sem, mark_at(L, ("pooled", j)))
                            for h in range(2):
                                name = ("pm", j, h)
                                pe.wait_ge(aux_read(name), aux_free_at(L, name))
                                pe.matmul(abank(name), par[:, A_PW + P * j:A_PW + P * j + P],
                                                   mix[:, 3 + j, hs(h)], start=True, stop=True).then_inc(aux_done.sem, 1)
                    elif what == "rope":
                        p = args[0]
                        for w, nm in enumerate(("pq", "pk")):
                            for h in range(2):
                                pe.wait_ge(emptied[bank(U_RET + 3 * p + w, h)].sem, emptied_at(L, U_RET + 3 * p + w, h))
                                pe.wait_ge(aux_read((nm, p, h)), aux_free_at(L, (nm, p, h)))
                                pe.matmul(abank((nm, p, h)), const[:, C_PERM:C_PERM + P],
                                                   rqkv[:, p % 2, w, hs(h)], start=True, stop=True).then_inc(aux_done.sem, 1)
                    elif what == "turn":
                        p = args[0]
                        for h in range(2):
                            name = ("vt", p, h)
                            pe.wait_ge(emptied[bank(U_RET + 3 * p + 2, h)].sem, emptied_at(L, U_RET + 3 * p + 2, h))
                            pe.wait_ge(aux_read(name), aux_free_at(L, name))
                            for n in range(4):
                                o = HALF * h + P * n
                                ins = pe.transpose(abank(name)[:, P * n:P * n + P], rqkv[:, p % 2, 2, o:o + P], ident)
                            ins.then_inc(aux_done.sem, 1)
                        for h in range(2):
                            name = ("kz", p, h)
                            pe.wait_ge(vec_step.sem, mark_at(L, ("roped", p, 1, h)))
                            pe.wait_ge(aux_read(name), aux_free_at(L, name))
                            for n in range(4):
                                o = HALF * h + P * n
                                ins = pe.transpose(abank(name)[:, P * n:P * n + P], KR[:, o:o + P], ident)
                            ins.then_inc(aux_done.sem, 1)
                    elif what == "scores":
                        p = args[0]
                        for e in range(2):
                            r = slice(RD * e, RD * e + RD)
                            for h in range(2):
                                name = ("rs", p, e, h)
                                pe.wait_ge(aux_read(name), aux_free_at(L, name))
                                for n in range(4):
                                    o = HALF * h + P * n
                                    ins = pe.matmul(abank(name)[:, P * n:P * n + P], KR[r, o:o + P], QR[r, o:o + P],
                                                    start=True, stop=True)
                                ins.then_inc(aux_done.sem, 1)
                    elif what == "state":
                        p = args[0]
                        name = ("rkv", p)
                        pe.wait_ge(aux_read(("vt", p, 1)), aux_read_at(L, ("vt", p, 1)))
                        pe.wait_ge(aux_read(("kz", p, 1)), aux_read_at(L, ("kz", p, 1)))
                        pe.wait_ge(aux_read(name), aux_free_at(L, name))
                        for n in range(NCH):
                            for e in range(2):
                                o = P * n + RD * e
                                ins = pe.matmul(abank(name)[RD * e:RD * e + RD, RD * n:RD * n + RD], KZ[:, o:o + RD],
                                                VT[:, o:o + RD], start=True, stop=True)
                        ins.then_inc(aux_done.sem, 1)
                    elif what == "ret_y":
                        p = args[0]
                        pe.wait_ge(vec_step.sem, mark_at(L, ("q_xi", p)))
                        for h in range(2):
                            name = ("ry", p, h)
                            pe.wait_ge(aux_read(("rs", p, 0, h)), aux_read_at(L, ("rs", p, 0, h)))
                            pe.wait_ge(aux_read(("rs", p, 1, h)), aux_read_at(L, ("rs", p, 1, h)))
                            pe.wait_ge(aux_read(("rkv", p)), aux_read_at(L, ("rkv", p)))
                            pe.wait_ge(aux_read(name), aux_free_at(L, name))
                            for n in range(4 * h, 4 * h + 4):
                                for e in range(2):
                                    r = slice(RD * e, RD * e + RD)
                                    out = abank(name)[r, P * (n % 4):P * (n % 4) + P]
                                    s = SC0[:, P * n:P * n + P] if e == 0 else sc1[:, n, :]
                                    pe.matmul(out, VT[:, P * n + RD * e:P * n + RD * e + RD], s, start=True, stop=False)
                                    ins = pe.matmul(out, rst[r, n, :], QX[r, P * n:P * n + P], start=False, stop=True)
                            ins.then_inc(aux_done.sem, 1)
                    elif what == "centre":
                        p = args[0]
                        for h in range(2):
                            name = ("rc", p, h)
                            pe.wait_ge(aux_read(("ry", p, h)), aux_read_at(L, ("ry", p, h)))
                            pe.wait_ge(aux_read(name), aux_free_at(L, name))
                            pe.matmul(abank(name), const[:, C_CEN:C_CEN + P], T0[:, hs(h)], start=True, stop=True).then_inc(aux_done.sem, 1)
                    elif what == "spread":
                        p = args[0]
                        for h in range(2):
                            name = ("rv", p, h)
                            pe.wait_ge(ret_sq.sem, ret_sq.at(L, 2 * p + h + 1))
                            pe.wait_ge(aux_read(name), aux_free_at(L, name))
                            pe.matmul(abank(name), const[:, C_MEAN:C_MEAN + P], QX[:, hs(h)], start=True, stop=True).then_inc(aux_done.sem, 1)
                    elif what == "out_units":
                        for m in range(8):
                            for h in range(2):
                                ready = None
                                if m == 0:
                                    ready = lambda i, k, h=h: pe.wait_ge(h_ready.sem, h_ready.at(L, 8 * h + i + 1))
                                narrow(L, U_OUT + m, h, MIX_ORDER, ready)
                    elif what == "norm":
                        i = args[0]
                        sums(L, 16 * i, i)
                        spread_rstd(L, 2 * i, i)
                    elif what == "ffn":
                        def up(u, g, lp, first=False):
                            for f in range(4):
                                for h in range(2):
                                    ready = None
                                    if first and f == 0:
                                        ready = lambda i, k, h=h: pe.wait_ge(h_ready.sem, h_ready.at(L, 16 + 8 * h + k + 1))
                                    narrow(L, u + f, h, ready=ready, fills=lp.fills, units=lp.units)

                        def down(u, g, lp):
                            pe.wait_ge(act_ready.sem, act_ready.at(L, lp.acts + (4 * g + 4)))
                            for k in range(16):
                                wide(L, u + k // 8, k % 8, ahi[:, g % 2], alo[:, g % 2], lp.fills, lp.units)

                        up(U_FFN, 0, LoopValues(0), True)
                        with pe.Fori(0, FG // 2) as i:
                            lp = LoopValues(i)
                            up(U_FFN + 4, 1, lp)
                            down(U_FFN + 8, 0, lp)
                            up(U_FFN + 10, 2, lp)
                            down(U_FFN + 14, 1, lp)
                        down(U_PROJ - 2, FG - 1, LoopValues(0))
                    elif what == "ple_proj":
                        pe.wait_ge(p_ready.sem, p_ready.at(L, 2))
                        for k in range(16):
                            wide(L, U_PROJ + k // 8, k % 8, phi[:, :, :], plo[:, :, :])
                            if k == 7:
                                sums(L, 16, 1)
                            if k == 11:
                                spread_rstd(L, 2, 1)
                    elif what == "ple_gate":
                        for m in range(8):
                            for h in range(2):
                                ready = None
                                if m == 0:
                                    ready = lambda i, k, h=h: pe.wait_ge(h_ready.sem, h_ready.at(L, 32 + 8 * h + k + 1))
                                narrow(L, U_GATE + m, h, ready=ready)


def constants():
    c = np.zeros((P, C_ALL), np.float64)
    i = np.arange(P)
    c[:, C_ID:C_ID + P] = np.eye(P)
    c[:, C_ONE:C_ONE + P] = 1.0
    for m in range(P):
        if m % RD < RD // 2:
            c[m + RD // 2, C_PERM + m] = -1.0
        else:
            c[m - RD // 2, C_PERM + m] = 1.0
    same = (i[:, None] // RD == i[None, :] // RD) / float(RD)
    c[:, C_CEN:C_CEN + P] = np.eye(P) - same
    c[:, C_MEAN:C_MEAN + P] = same
    c[:, C_NEG:C_NEG + P] = np.where(i[:, None] <= i[None, :], 0.0, -1e30)
    gamma = 1.0 - 2.0 ** (-5.0 - np.arange(RH))
    for h in range(RH):
        rel = i[None, :] - i[:, None]
        c[:, C_DEC + P * h:C_DEC + P * h + P] = np.where(rel >= 0, RSCALE * gamma[h] ** np.maximum(rel, 0), 0.0)
        c[:, C_ZETA + h] = RSCALE * gamma[h] ** (CHUNK - 1 - i)
    for p in range(PAIRS):
        g = gamma[2 * p + i // RD]
        c[:, C_XI + P * p:C_XI + P * p + P] = g[:, None] ** (i[None, :] + 1)
        c[:, C_GAM + p] = g ** CHUNK
    for h in range(MH):
        c[32 + h, C_SEL + P * h:C_SEL + P * h + P] = 1.0
    half = RD // 2
    c[:, C_FREQ] = 10000.0 ** (-(i % half) / half)
    for j in range(2):
        w = np.array([2.0, 4.0, 8.0, 16.0])[2 * j + i // 64]
        c[:, C_INVC + 16 * j:C_INVC + 16 * j + 16] = 1.0 / np.minimum(np.arange(1, 17)[None, :], w[:, None])
        c[:, C_INVW + j] = 1.0 / w
    for b, (_, _, first, last) in enumerate(BLOCKS):
        c[first:last, C_BLK + b] = 1.0
    return c.astype(np.float32)


def by_partition(a):
    return np.ascontiguousarray(np.moveaxis(a.reshape((-1, P) + a.shape[1:]), 0, 1))


def pack_weights(w_in, w_out, w_gate_up, w_down, w_ple_gate, w_ple_proj):
    out = np.zeros((UNITS, P, 1024), np.float32)

    def narrow(u, w, col):
        out[u] = by_partition(w[:, col:col + P]).reshape(P, 1024)

    def wide(u, w, row, col):
        out[u] = by_partition(w[row:row + 2 * P, col:col + HALF]).reshape(P, 1024)

    rq, rk, rv, rg, pu, mq, mk, mv, mo, mi, mf = np.cumsum([0] + [RW] * 4 + [PW] + [MW] * 4 + [MH])
    gates = out[U_GATES].reshape(P, KC, P)
    gates[:, :, 0:MH] = by_partition(w_in[:, mi:mi + MH])
    gates[:, :, 32:32 + MH] = by_partition(w_in[:, mf:mf + MH])
    for u0, o in ((U_MQ, mq), (U_MK, mk), (U_MV, mv), (U_MO, mo), (U_RG, rg)):
        for j in range(3):
            narrow(u0 + j, w_in, o + P * j)
    for j in range(2):
        narrow(U_POOL + j, w_in, pu + P * j)
    for p in range(PAIRS):
        for w, o in enumerate((rq, rk, rv)):
            narrow(U_RET + 3 * p + w, w_in, o + P * p)
    for m in range(8):
        narrow(U_OUT + m, w_out, P * m)
        narrow(U_GATE + m, w_ple_gate, P * m)

    def up(u, g):
        for f in range(2):
            narrow(u + 2 * f, w_gate_up, P * (2 * g + f))
            narrow(u + 2 * f + 1, w_gate_up, DFF + P * (2 * g + f))

    def down(u, g):
        for m in range(2):
            wide(u + m, w_down, 2 * P * g, HALF * m)

    up(U_FFN, 0)
    for g in range(1, FG):
        up(U_FFN + 6 * g - 2, g)
        down(U_FFN + 6 * g + 2, g - 1)
    down(U_PROJ - 2, FG - 1)
    for m in range(2):
        wide(U_PROJ + m, w_ple_proj, 0, HALF * m)
    return out


def kernel(x, p, positions, norm_mix, w_in, ret_gn, pool_w, pool_scale, conv_w, conv_b, b_igate, b_fgate,
           mlstm_gn, w_out, norm_ffn, w_gate_up, w_down, norm_ple, w_ple_gate, w_ple_proj, norm_final):
    import concourse.bacc as bacc
    from concourse.bass_utils import run_bass_kernel_spmd

    f = lambda a: np.asarray(a)
    weights = np.concatenate([pack_weights(f(w_in)[i], f(w_out)[i], f(w_gate_up)[i], f(w_down)[i],
                                           f(w_ple_gate)[i], f(w_ple_proj)[i]) for i in range(DEPTH)])
    par = np.zeros((DEPTH, P, A_ALL), np.float32)
    for i in range(DEPTH):
        par[i, :, A_FFN:A_FFN + 8] = by_partition(f(norm_ffn)[i])
        par[i, :, A_PLE:A_PLE + 8] = by_partition(f(norm_ple)[i])
        after = f(norm_mix)[i + 1] if i + 1 < DEPTH else f(norm_final)
        par[i, :, A_NEXT:A_NEXT + 8] = by_partition(after)
        par[i, :, A_CW:A_CW + 6 * CONV] = by_partition(f(conv_w)[i].T).reshape(P, 6 * CONV)
        par[i, :, A_CB:A_CB + 6] = by_partition(f(conv_b)[i])
        par[i, 0:MH, A_GB] = f(b_igate)[i]
        par[i, 32:32 + MH, A_GB] = f(b_fgate)[i]
        par[i, :, A_RG:A_RG + PAIRS] = by_partition(f(ret_gn)[i])
        par[i, :, A_PS:A_PS + 2] = by_partition(f(pool_scale)[i])
        par[i, :, A_MG:A_MG + MC] = by_partition(f(mlstm_gn)[i])
        for g in range(4):
            j, e = divmod(g, 2)
            par[i, 64 * e:64 * e + 64, A_PW + P * j + 64 * e:A_PW + P * j + 64 * e + 64] = f(pool_w)[i, g]
    arrays = {
        "weights": weights,
        "x_in": by_partition(np.ascontiguousarray(f(x)[0].T)),
        "p_in": np.stack([by_partition(np.ascontiguousarray(f(p)[i, 0].T)) for i in range(DEPTH)]),
        "positions_in": np.ascontiguousarray(f(positions)[0]),
        "constants": constants(),
        "parameters": par,
        "gain_first": by_partition(f(norm_mix)[0]),
    }
    nc = bacc.Bacc("TRN2", target_bir_lowering=False, num_devices=1, dynamic_dma_scratch_size=1024)
    args = [nc.dram_tensor(n, a.shape, mybir.dt.from_np(a.dtype), kind="ExternalInput").ap() for n, a in arrays.items()]
    out = nc.dram_tensor("out", (P, KC, S), F32, kind="ExternalOutput").ap()
    build(nc, *args, out)
    r = run_bass_kernel_spmd(nc, [arrays], core_ids=[0])
    y = np.asarray(r.results[0]["out"])
    return np.ascontiguousarray(y.transpose(1, 0, 2).reshape(D, S).T)[None]
```

```python
from contextlib import ExitStack

import numpy as np

import concourse.bass as bass
from concourse import mybir

F32 = mybir.dt.float32
F32R = mybir.dt.float32r
I32 = mybir.dt.int32
ACT = mybir.ActivationFunctionType
ALU = mybir.AluOpType
AX = mybir.AxisListType

P = 128
D = 1024
S = 1024
HALF = 512
DEPTH = 2
KC = D // P
PLE = 256
RH, RD = 6, 64
RW = RH * RD
PAIRS = RW // P
PW = 256
MH, MD = 4, 96
MW = MH * MD
MC = MW // P
CONV = 4
CHUNK = 128
NCH = S // CHUNK
DFF = 2816
FG = DFF // (2 * P)
EPS = 1e-6
MSCALE = float(MD) ** -0.5
RSCALE = float(RD) ** -0.5

U_GATES, U_MQ, U_MK, U_MV, U_MO, U_RG, U_POOL, U_RET, U_OUT, U_FFN = 0, 1, 4, 7, 10, 13, 16, 18, 27, 35
U_PROJ = U_FFN + 6 * FG
U_GATE = U_PROJ + 2
UNITS = U_GATE + 8
RAW, RING = 2, 3
assert UNITS % RING == 0 and DEPTH * UNITS % (RAW * RING) == 0

BLOCKS = [(0, 0, 0, 96), (1, 0, 96, 128), (1, 1, 0, 64), (2, 1, 64, 128), (2, 2, 0, 32), (3, 2, 32, 128)]
NB = len(BLOCKS)
MIX_ORDER = [5, 6, 7, 3, 4, 0, 1, 2]
EARLY = MIX_ORDER[:-1]

C_ID, C_ONE, C_PERM, C_CEN, C_MEAN, C_NEG = [i * P for i in range(6)]
C_DEC = 6 * P
C_XI = C_DEC + RH * P
C_SEL = C_XI + PAIRS * P
C_ZETA = C_SEL + MH * P
C_GAM = C_ZETA + RH
C_INVC = C_GAM + PAIRS
C_INVW = C_INVC + 2 * 16
C_BLK = C_INVW + 2
C_PART = C_BLK + NB
C_ALL = C_PART + 1

A_FFN, A_PLE, A_NEXT = 0, 8, 16
A_CW = 24
A_CB = A_CW + 6 * CONV
A_GB = A_CB + 6
A_RG = A_GB + 1
A_PS = A_RG + PAIRS
A_MG = A_PS + 2
A_PW = A_MG + MC
A_ALL = A_PW + 2 * P


def macro_schedule():
    m = [("norm",)] + [("unit", u) for u in range(U_MO)] + [("half", U_MO, 0), ("ml_cols",), ("half", U_MO, 1)]
    for n in range(NCH):
        m.append(("ml_a", n))
        if n < NCH - 1:
            m.append(("half", U_MO + n + 1, 0))
        m.append(("ml_b", n))
        if n < NCH - 1:
            m.append(("half", U_MO + n + 1, 1))
    m += [("gate_funcs",), ("ml_norm",), ("unit", U_RET), ("ml_fin",), ("pool_sums",), ("unit", U_RET + 1),
          ("unit", U_RET + 2), ("pool",)]
    for p in range(PAIRS - 1):
        for i, step in enumerate(("rope", "turn", "scores", "state", "ret_y", "spread")):
            m.append((step, p))
            if not (p == PAIRS - 2 and i == 5):
                m.append(("half", U_RET + 3 * (p + 1) + i // 2, i % 2))
    p = PAIRS - 1
    m += [("rope", p), ("half", U_OUT - 1, 1), ("early_high",), ("turn", p), ("early_low", 0), ("scores", p),
          ("out_part", 0), ("state", p), ("early_low", 1), ("out_part", 2), ("ret_y", p), ("spread", p),
          ("out_part", 1), ("out_part", 3)]
    m += [("mix_split",), ("out_units",), ("ffn",), ("ple_proj",), ("ple_gate",)]
    return m


MACRO = macro_schedule()


def unit_fills(u):
    return 8 if is_wide(u) else 2


def is_wide(u):
    if U_FFN + 4 <= u < U_PROJ - 2:
        return (u - U_FFN - 4) % 6 >= 4
    return U_PROJ - 2 <= u < U_GATE


FILL0 = [sum(unit_fills(v) for v in range(u)) for u in range(UNITS + 1)]
FILLS = FILL0[UNITS]
FILLS_TOLD = FILLS - UNITS

STAGE_FILLS = {
    "ml_cols": lambda *a: [(("tt", b), b) for b in range(4)] + [(("so",), 0)],
    "ml_a": lambda n: [(("tk", n), 0), (("tv", n), 1), (("mb", n), 2), (("ms", n), 3)],
    "ml_b": lambda n: [(("num", n), 0), (("int", n), 1)] + ([(("kv0", n), 2), (("kv1", n), 3)] if n < NCH - 1 else []),
    "ml_fin": lambda *a: [(("yt", j, h), (2 * j + h) % 4) for j in range(MC) for h in range(2)],
    "pool": lambda *a: [(("pm", j, h), 2 * j + h) for j in range(2) for h in range(2)],
    "rope": lambda p: [(("pk", p, 0), 0), (("pk", p, 1), 1), (("pq", p, 0), 2), (("pq", p, 1), 3)],
    "turn": lambda p: [(("kz", p, 0), 0), (("kz", p, 1), 1), (("vt", p, 0), 2), (("vt", p, 1), 3)],
    "scores": lambda p: [(("rs", p, e, h), 2 * e + h) for e in range(2) for h in range(2)],
    "state": lambda p: [(("rkv", p), 0)],
    "ret_y": lambda p: [(("ry", p, h), 1 + h) for h in range(2)],
    "spread": lambda p: [(("rv", p, 0), 3), (("rv", p, 1), 0)],
}


NORMS = {"norm": 0, "ffn": 1, "ple_proj": 2}


def norm_fills(i):
    return [(("sum", i, 0), 0), (("sum", i, 1), 1), (("row", i, 0), 2), (("row", i, 1), 3)]


def plan_aux():
    table, order, per_bank = {}, 0, [0] * 4
    for item in MACRO:
        if item[0] in NORMS:
            fills = norm_fills(NORMS[item[0]])
        elif item[0] in STAGE_FILLS:
            fills = STAGE_FILLS[item[0]](*item[1:])
        else:
            continue
        for name, bank in fills:
            table[name] = (bank, order, per_bank[bank])
            order += 1
            per_bank[bank] += 1
    return table, order, per_bank


AUX, AUX_FILLS, AUX_PER_BANK = plan_aux()
VEC_STEPS = 348


PRE_VEC = 20


class LoopValues:

    def __init__(self, i):
        self.units, self.acts, self.told = i * 12, i * 8, i * 36
        self.fills = i * 12


class Signal:

    def __init__(self, sem, per_layer, start=0):
        self.sem, self.per_layer, self.start = sem, per_layer, start

    def at(self, layer, k):
        return layer * self.per_layer + (k + self.start)


def build(nc, w_d, x_d, p_d, pos_d, const_d, par_d, early_d, out_d):
    spill_d = nc.dram_tensor("x_spill", (P, KC, S), F32, kind="Internal").ap()
    with ExitStack() as ctx:
        def sb(name, shape, dt=F32):
            return ctx.enter_context(nc.sbuf_tensor(name, shape, dt))[:]

        def sem(name):
            return ctx.enter_context(nc.semaphore(name))

        hh = sb("h_hi", [P, KC, S], F32R)
        hl = sb("h_lo", [P, KC, S], F32R)
        raw = sb("w_raw", [P, RAW, 1024])
        whi = sb("w_hi", [P, RING, 1024], F32R)
        wlo = sb("w_lo", [P, RING, 1024], F32R)
        const = sb("const", [P, C_ALL])
        par = sb("par", [P, A_ALL])
        early = sb("early", [P, KC + 1])
        mix_gain = early[:, 0:KC]
        rstd = sb("rstd", [P, 2, HALF])
        cosT = sb("cosT", [P, S])
        sinT = sb("sinT", [P, S])
        rows = sb("rows", [P, 2, S])
        small = sb("small", [P, 64])
        zero1 = sb("zero1", [P, 1])
        XB = 4 * KC * S
        WB = 30720
        arena_at = -(-nc.sbuf_base // 64) * 64
        sb("arena", [P, (2 * XB + WB + 64) // 4])
        x_at, mix_at, w_at = arena_at, arena_at + XB, arena_at + 2 * XB

        def at(name, offset, shape, dt=F32):
            return nc.alloc_sbuf_tensor_at(name, shape, dt, offset=offset)[:]

        x = at("x", x_at, [P, KC, S])
        mix = at("mix", mix_at, [P, KC, S])
        ahi = at("act_hi", mix_at, [P, 2, 2, S], F32R)
        alo = at("act_lo", mix_at + 4 * 4 * S, [P, 2, 2, S], F32R)
        pp = at("ple_in", mix_at, [P, KC, S])
        qk = at("ml_qk", x_at, [P, 6, S])
        gw = 4 * S
        t_at = x_at + 6 * gw
        dmat = at("ml_d", t_at, [P, MH, P])
        smat = at("ml_s", t_at + 2048, [P, MH, P])
        num = at("ml_num", t_at + 4096, [P, MH, MD + 1])
        tnum = at("ml_tmp", t_at + 5664, [P, MH, MD + 1])
        pool_t = at("pool_t", t_at, [P, 2, S])
        vm = at("ml_v", w_at, [P, NCH, MW])
        convraw = at("conv_raw", w_at + 12288, [P, 2, S + CONV - 1])
        kw = at("ml_kw", w_at + 12288, [P, NB, P])
        cst = at("ml_c", w_at + 15360, [P, 2, NB, MD + 1])
        tt = at("ml_cols", w_at + 20032, [P, NCH, 5, MH])
        so6 = at("ml_so", w_at + 20672, [P, NB, NCH])
        vx = at("ml_vx", w_at + 20864, [P, 2, MH, MD + 1])
        km = at("ml_km", w_at + 23968, [P, 2, NB, P])
        rqkv = at("ret_qkv", x_at, [P, 2, 3, S])
        sc1 = at("ret_s1", t_at, [P, NCH, P])
        rst = at("ret_state", t_at + gw, [P, NCH, RD])
        rw = [at(f"ret_t{i}", w_at + gw * i, [P, S]) for i in range(7)]
        sqr = at("squares", w_at, [P, 2, HALF])
        silu_g = at("silu_g", w_at, [P, 2, HALF])
        acc = at("square_sum", w_at + 4096, [P, 2, HALF])
        act_t = at("act", w_at + 4096, [P, 2, HALF])
        diag = at("diag", w_at + 8192, [P, 4, P])
        praw = at("p_raw", w_at + 22528, [P, 2, S])
        phi = at("p_hi", w_at + 14336, [P, 2, S], F32R)
        plo = at("p_lo", w_at + 22528, [P, 2, S], F32R)
        psg = at("ple_sig", w_at + 14336, [P, 2, HALF])
        pt = at("ple_t", w_at + 14336 + 4096, [P, 2, HALF])
        ang = at("ang", mix_at, [P, 4, HALF])
        posi = at("posi", mix_at + 5 * gw, [P, HALF], I32)

        proj = ctx.enter_context(nc.psum_tensor("proj", [P, 4, HALF], F32))
        aux = ctx.enter_context(nc.psum_tensor("aux", [P, 4, HALF], F32))

        ident = const[:, C_ID:C_ID + P]
        ones = const[:, C_ONE:C_ONE + P]
        eps_c, one_c = small[:, 0:1], small[:, 1:2]
        mprev = small[0:MH, 8:8 + NCH]
        rt_c, rc_c = small[:, 16:24], small[:, 24:32]
        den_c, mean_c = small[:, 32:36], small[:, 40:44]
        stat = sb("stat", [P, NCH, MH])
        tmp16 = sb("tmp16", [P, 16])

        const_landed, pos_landed = sem("const_landed"), sem("pos_landed")
        x_landed = [sem(f"x_landed{c}") for c in range(KC)]
        par_landed, spilled, reloaded, p_landed = sem("par_landed"), sem("spilled"), [sem(f"reloaded{i}") for i in range(3)], sem("p_landed")
        out_stored = sem("out_stored")
        early_landed = sem("early_landed")
        gains_kept = sem("gains_kept")
        raw_landed = [sem(f"raw_landed{r}") for r in range(RAW)]
        w_hi_made = sem("w_hi_made")
        weights_ready = Signal(sem("weights_ready"), UNITS, RING)
        unit_done = Signal(sem("unit_done"), UNITS, RING)
        fill_done = Signal(sem("fill_done"), FILLS_TOLD)
        emptied = [Signal(sem(f"proj_emptied{b}"), len(range(b, FILLS, 4)), 1) for b in range(4)]
        aux_done = Signal(sem("aux_done"), AUX_FILLS)
        aux_emptied = [Signal(sem(f"aux_emptied{b}"), AUX_PER_BANK[b], 1) for b in range(4)]
        sq_made = Signal(sem("sq_made"), 48, 16)
        sq_added = Signal(sem("sq_added"), 48, 16)
        diag_made = Signal(sem("diag_made"), 6)
        h_hi = Signal(sem("h_hi_made"), 64)
        h_ready = Signal(sem("h_ready"), 64)
        silu_made = Signal(sem("qk_ready"), 6)
        row_act = Signal(sem("row_funcs"), 5)
        d_exp = Signal(sem("d_exp"), NCH)
        gated = Signal(sem("gate_funcs"), 6)
        rc_sig = Signal(sem("token_rstd"), 6)
        ml_rt = Signal(sem("ml_root"), 1)
        ret_rstd = Signal(sem("ret_rstd"), 2 * PAIRS)
        ret_sq = Signal(sem("ret_squares"), 2 * PAIRS)
        p_hi_made = Signal(sem("p_hi_made"), 2)
        p_ready = Signal(sem("p_ready"), 2)
        act_hi_made = Signal(sem("act_hi_made"), 4 * FG)
        act_ready = Signal(sem("act_ready"), 4 * FG)
        ffn_silu = Signal(sem("ffn_silu"), 4 * FG)
        act_made = Signal(sem("act_made"), 4 * FG)
        ple_sig = Signal(sem("ple_sigmoid"), 16)
        trig_spread = sem("trig_spread")
        result = sem("result")
        x_ple = Signal(sem("x_ple"), 16)
        vec_step = Signal(sem("vec_step"), VEC_STEPS)
        pre_vec, pre_act = sem("pre_vec"), sem("pre_act")

        block = ctx.enter_context(nc.Block())
        marks = {}

        def bank(u, k):
            return (FILL0[u] + k) % 4

        def filled(u, k):
            return unit_done.sem if k == unit_fills(u) - 1 else fill_done.sem

        def filled_at(L, u, k, more=0, more_units=0):
            if k == unit_fills(u) - 1:
                return unit_done.at(L, more_units + (u + 1))
            return fill_done.at(L, more + (FILL0[u] - u + k + 1))

        def emptied_at(L, u, k, more=0):
            return emptied[bank(u, k)].at(L, more + ((FILL0[u] + k) // 4 + 1))

        def free_at(L, u, k, more=0):
            return emptied[bank(u, k)].at(L, more + (FILL0[u] + k) // 4)

        def aux_at(L, name):
            return aux_done.at(L, AUX[name][1] + 1)

        def aux_read(name):
            return aux_emptied[AUX[name][0]].sem

        def aux_read_at(L, name):
            return aux_emptied[AUX[name][0]].at(L, AUX[name][2] + 1)

        def aux_free_at(L, name):
            return aux_emptied[AUX[name][0]].at(L, AUX[name][2])

        def mark_at(L, name):
            return vec_step.at(L, marks[name])

        def pbank(u, k):
            return proj[:, (FILL0[u] + k) % 4, :]

        def abank(name):
            return aux[:, AUX[name][0], :]

        def hs(half):
            return slice(HALF * half, HALF * half + HALF)

        @block.vector
        def _(v):
            steps = [0]

            def count(mark=None):
                steps[0] += 1
                if mark is not None:
                    marks[mark] = steps[0]

            def step_at(L, mark=None):
                count(mark)
                return vec_step.at(L, steps[0])

            def norm_rows(L, i):
                for h in range(2):
                    v.wait_ge(aux_read(("sum", i, h)), aux_read_at(L, ("sum", i, h)))
                    v.reciprocal(rc_c[:, 4 * h:4 * h + 4], rt_c[:, 4 * h:4 * h + 4]).then_inc(rc_sig.sem, 1)
                    v.wait_ge(rc_sig.sem, rc_sig.at(L, 2 * i + h + 1))
                    if h == 1:
                        v.wait_ge(aux_done.sem, aux_at(L, ("row", i, 0)))
                    v.tensor_tensor(diag[:, :, :], ident.unsqueeze(1).to_broadcast([P, 4, P]),
                                    rc_c[:, 4 * h:4 * h + 4].unsqueeze(2).to_broadcast([P, 4, P]),
                                    ALU.mult).then_inc(diag_made.sem, 1)

            def low_part(L, k, c, h, gain):
                v.wait_ge(h_hi.sem, h_hi.at(L, k))
                v.scalar_tensor_tensor(hl[:, c, hs(h)], x[:, c, hs(h)], gain,
                                       hh[:, c, hs(h)].bitcast(F32), ALU.mult, ALU.subtract).then_inc(h_ready.sem, 1)

            def add_square(L, base, j):
                c, h = divmod(j, 2)
                v.wait_ge(sq_made.sem, sq_made.at(L, base + j + 1))
                if c == 0:
                    v.tensor_copy(acc[:, h, :], sqr[:, j % 2, :]).then_inc(sq_added.sem, 1)
                else:
                    v.wait_ge(sq_added.sem, sq_added.at(L, base + j - 1))
                    v.tensor_tensor(acc[:, h, :], acc[:, h, :], sqr[:, j % 2, :], ALU.add).then_inc(sq_added.sem, 1)

            v.memset(small[:, :], 0.0).then_inc(pre_vec, 1)
            v.memset(rows[:, :, :], 0.0).then_inc(pre_vec, 1)
            v.wait_ge(pre_vec, 2)
            v.memset(eps_c, EPS).then_inc(pre_vec, 1)
            v.memset(one_c, 1.0).then_inc(pre_vec, 1)
            v.sem_inc(emptied[0].sem, 1)
            v.sem_inc(emptied[1].sem, 1)
            v.sem_inc(emptied[2].sem, 1)
            v.sem_inc(emptied[3].sem, 1)
            v.sem_inc(gains_kept, 1)
            v.sem_inc(aux_emptied[0].sem, 1)
            v.sem_inc(aux_emptied[1].sem, 1)
            v.sem_inc(aux_emptied[2].sem, 1)
            v.sem_inc(aux_emptied[3].sem, 1)
            v.wait_ge(early_landed, 16)
            v.wait_ge(pos_landed, 32)
            n_pre = [4]

            def pre(ins):
                ins.then_inc(pre_vec, 1)
                n_pre[0] += 1
                v.wait_ge(pre_vec, n_pre[0])

            two_pi = 6.283185307179586
            c1 = 6.28125
            c2 = float(np.float32(np.round((two_pi - c1) * 2.0 ** 21) / 2.0 ** 21))
            c3 = float(np.float32(two_pi - c1 - c2))
            magic = 12582912.0
            pi_low = 3.1415925
            pre(v.tensor_copy(ang[:, 0, :], posi[:, :]))
            pre(v.tensor_scalar(ang[:, 0, :], ang[:, 0, :], early[:, KC:KC + 1], None, ALU.mult))
            for turn, (to, quarter_turn) in enumerate(((1, 0.0), (2, 0.25))):
                pre(v.tensor_scalar(ang[:, 3, :], ang[:, 0, :], 1.0 / two_pi, quarter_turn, ALU.mult, ALU.add))
                pre(v.tensor_scalar(ang[:, 3, :], ang[:, 3, :], magic, magic, ALU.add, ALU.subtract))
                pre(v.scalar_tensor_tensor(ang[:, to, :], ang[:, 3, :], -c1, ang[:, 0, :], ALU.mult, ALU.add))
                pre(v.scalar_tensor_tensor(ang[:, to, :], ang[:, 3, :], -c2, ang[:, to, :], ALU.mult, ALU.add))
                pre(v.scalar_tensor_tensor(ang[:, to, :], ang[:, 3, :], -c3, ang[:, to, :], ALU.mult, ALU.add))
                pre(v.tensor_scalar(ang[:, to, :], ang[:, to, :], quarter_turn * two_pi, pi_low, ALU.add, ALU.min))
                pre(v.tensor_scalar(ang[:, to, :], ang[:, to, :], -pi_low, None, ALU.max))
                for j in range(6 * turn, 6 + 10 * turn):
                    add_square(0, -16, j)
            assert n_pre[0] == PRE_VEC
            v.wait_ge(const_landed, 16)

            def evacuate(L, u, k):
                v.wait_ge(filled(u, k), filled_at(L, u, k))
                src, scale, sl = pbank(u, k), rstd[:, k, :], hs(k)
                if u == U_GATES:
                    src, scale, dst = src[0:64], scale[0:64], mix[0:64, 0, sl]
                elif u < U_MV:
                    dst = convraw[:, (u - U_MQ) % 2, CONV - 1 + HALF * k:CONV - 1 + HALF * k + HALF]
                elif u < U_MO:
                    j = u - U_MV
                    dst = vm[:, 4 * k:4 * k + 4, P * j:P * j + P]
                    src = src.rearrange("p (n c) -> p n c", c=P)
                    scale = scale.rearrange("p (n c) -> p n c", c=P)
                elif u < U_RG:
                    dst = mix[:, 5 + u - U_MO, sl]
                elif u < U_POOL:
                    dst = mix[:, u - U_RG, sl]
                elif u < U_RET:
                    dst = mix[:, 3 + u - U_POOL, sl]
                else:
                    p, w = divmod(u - U_RET, 3)
                    dst = rqkv[:, p % 2, w, sl]
                v.tensor_tensor(dst, src, scale, ALU.mult).then_inc(emptied[bank(u, k)].sem, 1)

            def conv(L, c):
                u = U_MQ + c
                if c == 0:
                    v.wait_ge(spilled, L * 16 + 16)
                v.wait_ge(emptied[bank(u, 0)].sem, emptied_at(L, u, 0))
                v.wait_ge(emptied[bank(u, 1)].sem, emptied_at(L, u, 1))
                r, dst = convraw[:, c % 2, :], qk[:, c, :]
                w = [par[:, A_CW + CONV * c + t:A_CW + CONV * c + t + 1] for t in range(CONV)]
                v.tensor_scalar(dst, r[:, 3:3 + S], w[3], par[:, A_CB + c:A_CB + c + 1], ALU.mult, ALU.add).then_inc(vec_step.sem, 1)
                v.wait_ge(vec_step.sem, step_at(L))
                for t in (2, 1, 0):
                    v.scalar_tensor_tensor(dst, r[:, t:t + S], w[t], dst, ALU.mult, ALU.add).then_inc(vec_step.sem, 1)
                    v.wait_ge(vec_step.sem, step_at(L, ("conv", c) if t == 0 else None))

            def running(L, src, bufs, op):
                for i in range(7):
                    sh, dst = 1 << i, bufs[i % 2]
                    a = src.rearrange("p (n c) -> p n c", c=CHUNK)
                    o = dst.rearrange("p (n c) -> p n c", c=CHUNK)
                    v.tensor_copy(o[:, :, 0:sh], a[:, :, 0:sh]).then_inc(vec_step.sem, 1)
                    count()
                    v.tensor_tensor(o[:, :, sh:], a[:, :, sh:], a[:, :, 0:CHUNK - sh], op).then_inc(vec_step.sem, 1)
                    v.wait_ge(vec_step.sem, step_at(L))
                    src = dst
                return src

            m_ = [mix[:, i, :] for i in range(5)]
            by_chunk = "p (n c) -> p n c"
            R4 = slice(0, MH)

            def gate_rows_1(L):
                v.wait_ge(emptied[bank(U_GATES, 0)].sem, emptied_at(L, U_GATES, 0))
                v.wait_ge(emptied[bank(U_GATES, 1)].sem, emptied_at(L, U_GATES, 1))
                v.tensor_scalar(m_[1][R4], m_[0][32:32 + MH], par[32:32 + MH, A_GB:A_GB + 1], None, ALU.add).then_inc(vec_step.sem, 1)
                v.wait_ge(vec_step.sem, step_at(L))
                v.scalar_tensor_tensor(m_[3][R4], m_[1][R4], -1.0, m_[1][R4], ALU.mult, ALU.min).then_inc(vec_step.sem, 1)
                v.wait_ge(vec_step.sem, step_at(L, "neg_abs"))

            def gate_rows_2(L):
                v.wait_ge(row_act.sem, row_act.at(L, 2))
                v.scalar_tensor_tensor(m_[2][R4], m_[1][R4], 0.0, m_[3][R4], ALU.min, ALU.subtract).then_inc(vec_step.sem, 1)
                v.wait_ge(vec_step.sem, step_at(L))
                running(L, m_[2][R4], [m_[3][R4], m_[4][R4]], ALU.add)

            def gate_rows_3(L):
                u, bc = rows[R4, 0, :], m_[3][R4]
                v.scalar_tensor_tensor(u, m_[0][R4], par[R4, A_GB:A_GB + 1], bc, ALU.add, ALU.subtract).then_inc(vec_step.sem, 1)
                v.wait_ge(vec_step.sem, step_at(L))
                running(L, u, [m_[4][R4], m_[2][R4]], ALU.max)

            def gate_rows_4(L):
                u, bc, cm = rows[R4, 0, :], m_[3][R4], m_[4][R4]
                bc3, cm3 = bc.rearrange(by_chunk, c=CHUNK), cm.rearrange(by_chunk, c=CHUNK)
                for n in range(NCH - 1):
                    v.scalar_tensor_tensor(mprev[:, n + 1:n + 2], mprev[:, n:n + 1], cm3[:, n, CHUNK - 1:],
                                           bc3[:, n, CHUNK - 1:], ALU.max, ALU.add).then_inc(vec_step.sem, 1)
                    v.wait_ge(vec_step.sem, step_at(L))
                mp = mprev.unsqueeze(2).to_broadcast([MH, NCH, CHUNK])
                big = m_[2][R4].rearrange(by_chunk, c=CHUNK)
                v.tensor_tensor(big, mp, cm3, ALU.max).then_inc(vec_step.sem, 1)
                v.wait_ge(vec_step.sem, step_at(L))
                v.tensor_scalar(rows[32:32 + MH, 0, :], m_[2][R4], -1.0, None, ALU.mult).then_inc(vec_step.sem, 1)
                v.wait_ge(vec_step.sem, step_at(L))
                v.tensor_tensor(m_[1][R4].rearrange(by_chunk, c=CHUNK), mp, big, ALU.subtract).then_inc(vec_step.sem, 1)
                v.wait_ge(vec_step.sem, step_at(L, "inter_log"))
                v.tensor_tensor(m_[4][R4], bc, m_[2][R4], ALU.add).then_inc(vec_step.sem, 1)
                v.wait_ge(vec_step.sem, step_at(L, "m_row"))
                v.tensor_tensor(m_[3][R4].rearrange(by_chunk, c=CHUNK), u.rearrange(by_chunk, c=CHUNK),
                                big[:, :, CHUNK - 1:].to_broadcast([MH, NCH, CHUNK]), ALU.subtract).then_inc(vec_step.sem, 1)
                v.wait_ge(vec_step.sem, step_at(L, "pw_log"))

            def gate_rows_5(L):
                v.wait_ge(row_act.sem, row_act.at(L, 3))
                v.tensor_scalar(rows[64:64 + MH, 0, :], m_[0][R4], MSCALE, None, ALU.mult).then_inc(vec_step.sem, 1)
                v.wait_ge(vec_step.sem, step_at(L))
                v.tensor_copy(rows[32:32 + MH, 1, 0:NCH],
                              m_[0][R4].rearrange(by_chunk, c=CHUNK)[:, :, CHUNK - 1]).then_inc(vec_step.sem, 1)
                v.wait_ge(vec_step.sem, step_at(L, "rows_end"))

            def key_blocks(L, n):
                if n >= 2:
                    v.wait_ge(aux_done.sem, aux_at(L, ("ms", n - 2)))
                for j in range(MC):
                    b = slice(2 * j, 2 * j + 2)
                    v.tensor_tensor(km[:, n % 2, b, :], qk[:, 3 + j:4 + j, P * n:P * n + P].to_broadcast([P, 2, P]),
                                    const[:, C_BLK + 2 * j:C_BLK + 2 * j + 2].unsqueeze(2).to_broadcast([P, 2, P]),
                                    ALU.mult).then_inc(vec_step.sem, 1)
                    count(("key_blocks", n))

            def ml_a(L, n):
                if n == 0:
                    v.wait_ge(silu_made.sem, silu_made.at(L, 6))
                    key_blocks(L, 0)
                    v.memset(kw[:, :, :], 0.0).then_inc(vec_step.sem, 1)
                    v.wait_ge(vec_step.sem, step_at(L))
                    v.memset(cst[:, 0, :, :], 0.0).then_inc(vec_step.sem, 1)
                    v.wait_ge(vec_step.sem, step_at(L, "c_zero"))
                    v.memset(vx[:, :, :, MD:MD + 1], 1.0).then_inc(vec_step.sem, 1)
                    v.wait_ge(vec_step.sem, step_at(L, "vx_ones"))
                    for b in range(4):
                        v.wait_ge(aux_read(("tt", b)), aux_read_at(L, ("tt", b)))
                    v.wait_ge(aux_read(("so",)), aux_read_at(L, ("so",)))
                v.wait_ge(aux_done.sem, aux_at(L, ("tk", n)))
                if n > 0:
                    v.wait_ge(aux_done.sem, aux_at(L, ("kv1", n - 1)))
                for b, (h, j, r0, r1) in enumerate(BLOCKS):
                    ins = v.tensor_scalar(kw[:, b, r0:r1], abank(("tk", n))[:, P * j + r0:P * j + r1],
                                          tt[:, n, 4, h:h + 1], None, ALU.mult)
                    if b < NB - 1:
                        ins.then_inc(vec_step.sem, 1)
                        count(("kw_first", n))
                    else:
                        ins.then_inc(aux_emptied[0].sem, 1)
                v.wait_ge(aux_done.sem, aux_at(L, ("mb", n)))
                mb = abank(("mb", n)).rearrange("p (h c) -> p h c", h=MH)
                if n < NCH - 1:
                    key_blocks(L, n + 1)
                for h in range(MH):
                    ins = v.scalar_tensor_tensor(dmat[:, h, :], mb[:, h, :], tt[:, n, 0, h:h + 1],
                                                 const[:, C_NEG:C_NEG + P], ALU.add, ALU.add)
                    if h < MH - 1:
                        ins.then_inc(vec_step.sem, 1)
                        count()
                    else:
                        ins.then_inc(aux_emptied[2].sem, 1)
                v.wait_ge(aux_done.sem, aux_at(L, ("ms", n)))
                v.wait_ge(d_exp.sem, d_exp.at(L, n + 1))
                v.scalar_tensor_tensor(smat.rearrange("p h c -> p (h c)"), abank(("ms", n)), MSCALE,
                                       dmat.rearrange("p h c -> p (h c)"), ALU.mult,
                                       ALU.mult).then_inc(aux_emptied[3].sem, 1)

            def ml_b(L, n):
                E = MD + 1
                v.wait_ge(aux_done.sem, aux_at(L, ("int", n)))
                v.tensor_tensor(tnum[:, :, :], abank(("int", n))[:, 0:MH * E].rearrange("p (h e) -> p h e", h=MH),
                                tt[:, n, 2, :].unsqueeze(2).to_broadcast([P, MH, E]),
                                ALU.mult).then_inc(aux_emptied[1].sem, 1)
                v.wait_ge(aux_read(("int", n)), aux_read_at(L, ("int", n)))
                v.tensor_tensor(num[:, :, :], abank(("num", n))[:, 0:MH * E].rearrange("p (h e) -> p h e", h=MH),
                                tnum[:, :, :], ALU.add).then_inc(aux_emptied[0].sem, 1)
                if n < NCH - 1:
                    a, b = cst[:, n % 2, :, :], cst[:, (n + 1) % 2, :, :]
                    if n > 0:
                        v.wait_ge(aux_read(("kv0", n - 1)), aux_read_at(L, ("kv0", n - 1)))
                        v.wait_ge(aux_read(("kv1", n - 1)), aux_read_at(L, ("kv1", n - 1)))
                    v.tensor_tensor(b, a, so6[:, :, n:n + 1].to_broadcast([P, NB, E]), ALU.mult).then_inc(vec_step.sem, 1)
                    v.wait_ge(vec_step.sem, step_at(L))
                    for i in range(2):
                        v.wait_ge(aux_done.sem, aux_at(L, (f"kv{i}", n)))
                        v.tensor_tensor(b[:, 3 * i:3 * i + 3, :], b[:, 3 * i:3 * i + 3, :],
                                        abank((f"kv{i}", n))[:, 0:3 * E].rearrange("p (b e) -> p b e", b=3),
                                        ALU.add).then_inc(aux_emptied[2 + i].sem, 1)
                v.wait_ge(aux_read(("num", n)), aux_read_at(L, ("num", n)))
                den3 = den_c.unsqueeze(2)
                v.scalar_tensor_tensor(den3, num[:, :, MD:E], -1.0, num[:, :, MD:E], ALU.mult, ALU.max).then_inc(vec_step.sem, 1)
                v.wait_ge(vec_step.sem, step_at(L))
                v.tensor_tensor(den_c, den_c, tt[:, n, 3, :], ALU.max).then_inc(vec_step.sem, 1)
                v.wait_ge(vec_step.sem, step_at(L))
                hx = vm[:, n, :].rearrange("p (h d) -> p h d", h=MH)
                v.reciprocal(den_c, den_c).then_inc(vec_step.sem, 1)
                v.wait_ge(vec_step.sem, step_at(L))
                v.tensor_tensor(hx, num[:, :, 0:MD], den_c.unsqueeze(2).to_broadcast([P, MH, MD]),
                                ALU.mult).then_inc(vec_step.sem, 1)
                v.wait_ge(vec_step.sem, step_at(L))
                v.tensor_reduce(mean_c, hx, AX.X, ALU.add).then_inc(vec_step.sem, 1)
                v.wait_ge(vec_step.sem, step_at(L))
                v.tensor_scalar(mean_c, mean_c, -1.0 / MD, None, ALU.mult).then_inc(vec_step.sem, 1)
                v.wait_ge(vec_step.sem, step_at(L))
                v.tensor_tensor(hx, hx, mean_c.unsqueeze(2).to_broadcast([P, MH, MD]), ALU.add).then_inc(vec_step.sem, 1)
                v.wait_ge(vec_step.sem, step_at(L))
                v.tensor_tensor(tnum[:, :, 0:MD], hx, hx, ALU.mult).then_inc(vec_step.sem, 1)
                v.wait_ge(vec_step.sem, step_at(L))
                v.tensor_reduce(stat[:, n, :], tnum[:, :, 0:MD], AX.X, ALU.add).then_inc(vec_step.sem, 1)
                v.wait_ge(vec_step.sem, step_at(L, ("ml_var", n)))

            def ml_norm(L):
                v.wait_ge(ml_rt.sem, ml_rt.at(L, 1))
                v.reciprocal(stat[:, :, :], stat[:, :, :]).then_inc(vec_step.sem, 1)
                v.wait_ge(vec_step.sem, step_at(L))
                for n in range(NCH):
                    hx = vm[:, n, :].rearrange("p (h d) -> p h d", h=MH)
                    v.tensor_tensor(hx, hx, stat[:, n, :].unsqueeze(2).to_broadcast([P, MH, MD]),
                                    ALU.mult).then_inc(vec_step.sem, 1)
                    count(("ml_y", n))

            def ml_fin(L):
                v.wait_ge(gated.sem, gated.at(L, 3))
                for j in range(MC):
                    for h in range(2):
                        name = ("yt", j, h)
                        v.wait_ge(aux_done.sem, aux_at(L, name))
                        o = mix[:, 5 + j, hs(h)]
                        v.scalar_tensor_tensor(o, abank(name), par[:, A_MG + j:A_MG + j + 1], o, ALU.mult,
                                               ALU.mult).then_inc(aux_read(name), 1)

            def shifted_add(L, dst, src, sh, r):
                v.tensor_copy(dst[r, 0:sh], src[r, 0:sh]).then_inc(vec_step.sem, 1)
                count()
                v.tensor_tensor(dst[r, sh:], src[r, sh:], src[r, 0:S - sh], ALU.add).then_inc(vec_step.sem, 1)
                v.wait_ge(vec_step.sem, step_at(L))

            def pool_sums(L):
                every, low, high = slice(0, P), slice(0, 64), slice(64, P)
                for j in range(2):
                    v.wait_ge(emptied[bank(U_POOL + j, 0)].sem, emptied_at(L, U_POOL + j, 0))
                    v.wait_ge(emptied[bank(U_POOL + j, 1)].sem, emptied_at(L, U_POOL + j, 1))
                    u, a, b = mix[:, 3 + j, :], pool_t[:, 0, :], pool_t[:, 1, :]
                    shifted_add(L, a, u, 1, every)
                    if j == 0:
                        shifted_add(L, b, a, 2, high)
                        v.tensor_copy(b[low], a[low]).then_inc(vec_step.sem, 1)
                        v.wait_ge(vec_step.sem, step_at(L))
                        win = b
                    else:
                        shifted_add(L, b, a, 2, every)
                        shifted_add(L, a, b, 4, every)
                        shifted_add(L, b, a, 8, high)
                        v.tensor_copy(b[low], a[low]).then_inc(vec_step.sem, 1)
                        v.wait_ge(vec_step.sem, step_at(L))
                        win = b
                    v.tensor_tensor(tmp16[:, :], win[:, 0:16],
                                    const[:, C_INVC + 16 * j:C_INVC + 16 * j + 16], ALU.mult).then_inc(vec_step.sem, 1)
                    v.wait_ge(vec_step.sem, step_at(L))
                    v.tensor_tensor(tmp16[:, :], tmp16[:, :], u[:, 0:16], ALU.subtract).then_inc(vec_step.sem, 1)
                    v.wait_ge(vec_step.sem, step_at(L))
                    v.scalar_tensor_tensor(u, win, const[:, C_INVW + j:C_INVW + j + 1], u, ALU.mult,
                                           ALU.subtract).then_inc(vec_step.sem, 1)
                    v.wait_ge(vec_step.sem, step_at(L))
                    v.tensor_copy(u[:, 0:16], tmp16[:, :]).then_inc(vec_step.sem, 1)
                    v.wait_ge(vec_step.sem, step_at(L, ("pooled", j)))

            T0, QR, KR, QX, VT, KZ, SC0 = rw

            def rope(L, p):
                b = p % 2
                if p == 0:
                    v.wait_ge(pre_act, 4)
                    v.wait_ge(trig_spread, 64)
                for which, name, dst in ((1, "pk", KR), (0, "pq", QR)):
                    u = U_RET + 3 * p + which
                    v.wait_ge(emptied[bank(u, 0)].sem, emptied_at(L, u, 0))
                    v.wait_ge(emptied[bank(u, 1)].sem, emptied_at(L, u, 1))
                    v.tensor_tensor(T0[:, :], rqkv[:, b, which, :], cosT[:, :], ALU.mult).then_inc(vec_step.sem, 1)
                    v.wait_ge(vec_step.sem, step_at(L, ("cos_part", p, which)))
                    for h in range(2):
                        v.wait_ge(aux_done.sem, aux_at(L, (name, p, h)))
                        v.tensor_tensor(dst[:, hs(h)], abank((name, p, h)), sinT[:, hs(h)],
                                        ALU.mult).then_inc(aux_emptied[AUX[(name, p, h)][0]].sem, 1)
                    for h in range(2):
                        v.wait_ge(aux_read((name, p, h)), aux_read_at(L, (name, p, h)))
                        v.tensor_tensor(dst[:, hs(h)], dst[:, hs(h)], T0[:, hs(h)], ALU.add).then_inc(vec_step.sem, 1)
                        v.wait_ge(vec_step.sem, step_at(L, ("roped", p, which, h)))

            def turn(L, p):
                for h in range(2):
                    name = ("kz", p, h)
                    v.wait_ge(aux_done.sem, aux_at(L, name))
                    src = abank(name).rearrange("p (n e d) -> p n e d", n=4, e=2)
                    dst = KZ[:, hs(h)].rearrange("p (n e d) -> p n e d", n=4, e=2)
                    for e in range(2):
                        ins = v.tensor_scalar(dst[:, :, e, :], src[:, :, e, :],
                                              const[:, C_ZETA + 2 * p + e:C_ZETA + 2 * p + e + 1], None, ALU.mult)
                        if e == 0:
                            ins.then_inc(vec_step.sem, 1)
                            count(("kz_first", p, h))
                        else:
                            ins.then_inc(aux_read(name), 1)

            def scores(L, p):
                xi = const[:, C_XI + P * p:C_XI + P * p + P].unsqueeze(1).to_broadcast([P, NCH, P])
                v.tensor_tensor(QX.rearrange("p (n c) -> p n c", c=P), QR.rearrange("p (n c) -> p n c", c=P),
                                xi, ALU.mult).then_inc(vec_step.sem, 1)
                count(("q_xi", p))
                for e in range(2):
                    dst = SC0.rearrange("p (n c) -> p n c", c=P) if e == 0 else sc1[:, :, :]
                    dec = const[:, C_DEC + P * (2 * p + e):C_DEC + P * (2 * p + e) + P].unsqueeze(1).to_broadcast([P, 4, P])
                    for h in range(2):
                        name = ("rs", p, e, h)
                        v.wait_ge(aux_done.sem, aux_at(L, name))
                        v.tensor_tensor(dst[:, 4 * h:4 * h + 4, :], abank(name).rearrange("p (n c) -> p n c", c=P),
                                        dec, ALU.mult).then_inc(aux_read(name), 1)

            def state(L, p):
                v.memset(rst[:, 0, :], 0.0).then_inc(vec_step.sem, 1)
                v.wait_ge(vec_step.sem, step_at(L))
                v.wait_ge(aux_done.sem, aux_at(L, ("rkv", p)))
                kvp = abank(("rkv", p)).rearrange("p (n d) -> p n d", n=NCH)
                for n in range(NCH - 1):
                    ins = v.scalar_tensor_tensor(rst[:, n + 1, :], rst[:, n, :], const[:, C_GAM + p:C_GAM + p + 1],
                                                 kvp[:, n, :], ALU.mult, ALU.add)
                    if n < NCH - 2:
                        ins.then_inc(vec_step.sem, 1)
                        v.wait_ge(vec_step.sem, step_at(L))
                    else:
                        ins.then_inc(aux_emptied[0].sem, 1)

            def spread(L, p):
                for h in range(2):
                    name = ("rv", p, h)
                    v.wait_ge(aux_read(("ry", p, h)), aux_read_at(L, ("ry", p, h)))
                    v.wait_ge(ret_rstd.sem, ret_rstd.at(L, 2 * p + h + 1))
                    v.scalar_tensor_tensor(T0[:, hs(h)], T0[:, hs(h)], par[:, A_RG + p:A_RG + p + 1],
                                           KZ[:, hs(h)], ALU.mult, ALU.mult).then_inc(vec_step.sem, 1)
                    v.wait_ge(vec_step.sem, step_at(L))
                    v.wait_ge(gated.sem, gated.at(L, 4 + p))
                    v.tensor_tensor(mix[:, p, hs(h)], mix[:, p, hs(h)], T0[:, hs(h)], ALU.mult).then_inc(vec_step.sem, 1)
                    v.wait_ge(vec_step.sem, step_at(L, ("ret_mix", p, h)))

            def mix_low(L, k, c, h):
                v.wait_ge(h_hi.sem, h_hi.at(L, 16 + k))
                v.tensor_tensor(hl[:, c, hs(h)], mix[:, c, hs(h)], hh[:, c, hs(h)].bitcast(F32),
                                ALU.subtract).then_inc(h_ready.sem, 1)

            def add_fill(L, u, k, m, h, more=0, more_units=0, told=0):
                v.wait_ge(filled(u, k), filled_at(L, u, k, told, more_units))
                v.tensor_tensor(x[:, m, hs(h)], x[:, m, hs(h)], pbank(u, k),
                                ALU.add).then_inc(emptied[bank(u, k)].sem, 1)

            def ffn_up(L, u, g, lp):
                for f in range(2):
                    ug, uu = u + 2 * f, u + 2 * f + 1
                    for h in range(2):
                        if not (type(lp.acts) is int and g == 0 and f == 0):
                            v.wait_ge(act_made.sem, act_made.at(L, lp.acts + (4 * g + 2 * f - 1 + h)))
                        v.wait_ge(filled(ug, h), filled_at(L, ug, h, lp.told, lp.units))
                        v.tensor_tensor(silu_g[:, h, :], pbank(ug, h), rstd[:, h, :],
                                        ALU.mult).then_inc(emptied[bank(ug, h)].sem, 1)
                    for h in range(2):
                        if not (type(lp.acts) is int and g == 0 and f == 0):
                            v.wait_ge(act_ready.sem, act_ready.at(L, lp.acts + (4 * g + 2 * f - 1 + h)))
                        v.wait_ge(filled(uu, h), filled_at(L, uu, h, lp.told, lp.units))
                        v.tensor_tensor(act_t[:, h, :], pbank(uu, h), rstd[:, h, :],
                                        ALU.mult).then_inc(emptied[bank(uu, h)].sem, 1)
                        v.wait_ge(ffn_silu.sem, ffn_silu.at(L, lp.acts + (4 * g + 2 * f + h + 1)))
                        v.wait_ge(emptied[bank(uu, h)].sem, emptied_at(L, uu, h, lp.fills))
                        v.tensor_tensor(act_t[:, h, :], act_t[:, h, :], silu_g[:, h, :],
                                        ALU.mult).then_inc(act_made.sem, 1)
                    for h in range(2):
                        v.wait_ge(act_hi_made.sem, act_hi_made.at(L, lp.acts + (4 * g + 2 * f + h + 1)))
                        v.wait_ge(act_made.sem, act_made.at(L, lp.acts + (4 * g + 2 * f + h + 1)))
                        v.tensor_tensor(alo[:, g % 2, f, hs(h)], act_t[:, h, :], ahi[:, g % 2, f, hs(h)].bitcast(F32),
                                        ALU.subtract).then_inc(act_ready.sem, 1)

            def ffn_down(L, u, lp, last):
                for k in range(16):
                    uu, kk = u + k // 8, k % 8
                    add_fill(L, uu, kk, k // 2, k % 2, 0, lp.units, lp.told)
                    if last and k >= 1:
                        add_square(L, 16, k - 1)
                if last:
                    add_square(L, 16, 15)
                    for j in range(16):
                        h, c = divmod(j, 8)
                        low_part(L, 48 + 2 * c + h + 1, c, h, par[:, A_PLE + c:A_PLE + c + 1])

            with v.Fori(0, DEPTH) as L:
                steps[0] = 0
                for item in MACRO:
                    what, args = item[0], item[1:]
                    if what == "norm":
                        for j in range(16):
                            h, c = divmod(j, 8)
                            low_part(L, j + 1, c, h, mix_gain[:, c:c + 1])
                        v.wait_ge(par_landed, L * 16 + 16)
                        v.memset(convraw[:, :, 0:CONV - 1], 0.0).then_inc(vec_step.sem, 1)
                        v.wait_ge(vec_step.sem, step_at(L))
                        norm_rows(L, 0)
                        for h in range(2):
                            v.wait_ge(aux_read(("row", 0, h)), aux_read_at(L, ("row", 0, h)))
                    elif what == "half":
                        evacuate(L, *args)
                    elif what == "unit":
                        evacuate(L, args[0], 0)
                        evacuate(L, args[0], 1)
                    if what == "unit" and U_MQ <= args[0] < U_MV:
                        if args[0] == U_MQ:
                            gate_rows_1(L)
                        conv(L, args[0] - U_MQ)
                        if args[0] == U_MQ + 1:
                            gate_rows_2(L)
                        elif args[0] == U_MQ + 3:
                            gate_rows_3(L)
                        elif args[0] == U_MQ + 5:
                            gate_rows_4(L)
                            gate_rows_5(L)
                    elif what == "ml_a":
                        ml_a(L, *args)
                    elif what == "ml_b":
                        ml_b(L, *args)
                    elif what == "ml_norm":
                        ml_norm(L)
                    elif what == "ml_fin":
                        ml_fin(L)
                    elif what == "pool_sums":
                        pool_sums(L)
                    elif what == "rope":
                        rope(L, *args)
                    elif what == "turn":
                        turn(L, *args)
                    elif what == "scores":
                        scores(L, *args)
                    elif what == "state":
                        state(L, *args)
                    elif what == "spread":
                        spread(L, *args)
                    elif what == "early_low":
                        h = args[0]
                        for i, c in enumerate(EARLY):
                            mix_low(L, 7 * h + i + 1, c, h)
                    elif what == "mix_split":
                        for h in range(2):
                            mix_low(L, 14 + h + 1, MIX_ORDER[7], h)
                    elif what == "out_units":
                        for part in reloaded:
                            v.wait_ge(part, L * 16 + 16)
                        for j in range(16):
                            add_fill(L, U_OUT + j // 2, j % 2, j // 2, j % 2)
                            if j >= 1:
                                add_square(L, 0, j - 1)
                            if j == 14:
                                for c in range(KC):
                                    low_part(L, 32 + c + 1, c, 0, par[:, A_FFN + c:A_FFN + c + 1])
                        add_square(L, 0, 15)
                        for c in range(KC):
                            low_part(L, 40 + c + 1, c, 1, par[:, A_FFN + c:A_FFN + c + 1])
                        norm_rows(L, 1)
                        for k in range(2):
                            v.wait_ge(p_hi_made.sem, p_hi_made.at(L, k + 1))
                            v.tensor_tensor(plo[:, k, :], praw[:, k, :], phi[:, k, :].bitcast(F32),
                                            ALU.subtract).then_inc(p_ready.sem, 1)
                        for h in range(2):
                            v.wait_ge(aux_read(("row", 1, h)), aux_read_at(L, ("row", 1, h)))
                    elif what == "ffn":
                        ffn_up(L, U_FFN, 0, LoopValues(0))
                        with v.Fori(0, FG // 2) as i:
                            lp = LoopValues(i)
                            ffn_up(L, U_FFN + 4, 1, lp)
                            ffn_down(L, U_FFN + 8, lp, False)
                            ffn_up(L, U_FFN + 10, 2, lp)
                            ffn_down(L, U_FFN + 14, lp, False)
                        ffn_down(L, U_PROJ - 2, LoopValues(0), True)
                    elif what == "ple_proj":
                        norm_rows(L, 2)
                        for h in range(2):
                            v.wait_ge(aux_read(("row", 2, h)), aux_read_at(L, ("row", 2, h)))
                    elif what == "ple_gate":
                        for j in range(16 + 2):
                            if j < 16:
                                m, h = divmod(j, 2)
                                v.wait_ge(filled(U_GATE + m, h), filled_at(L, U_GATE + m, h))
                                v.tensor_tensor(psg[:, h, :], pbank(U_GATE + m, h), rstd[:, h, :],
                                                ALU.mult).then_inc(emptied[bank(U_GATE + m, h)].sem, 1)
                            if 1 <= j < 17:
                                m, h = divmod(j - 1, 2)
                                v.wait_ge(ple_sig.sem, ple_sig.at(L, j))
                                v.tensor_tensor(pt[:, h, :], psg[:, h, :], pp[:, m, hs(h)],
                                                ALU.mult).then_inc(vec_step.sem, 1)
                                v.wait_ge(vec_step.sem, step_at(L))
                                v.tensor_tensor(x[:, m, hs(h)], x[:, m, hs(h)], pt[:, h, :],
                                                ALU.add).then_inc(x_ple.sem, 1)
                            if j >= 2:
                                add_square(L, 32, j - 2)
                assert steps[0] == VEC_STEPS, steps[0]
            norm_rows(DEPTH, 0)
            for j in range(16):
                h, c = divmod(j, 8)
                if c == 0:
                    v.wait_ge(aux_read(("row", 0, h)), aux_read_at(DEPTH, ("row", 0, h)))
                v.scalar_tensor_tensor(x[:, c, hs(h)], x[:, c, hs(h)], mix_gain[:, c:c + 1], rstd[:, h, :],
                                       ALU.mult, ALU.mult).then_inc(result, 1)

        @block.scalar
        def _(a):
            def square(L, base, j, final):
                c, h = divmod(j, 2)
                final(c, h, j)
                if not (type(L) is int and base + j + 16 < 2):
                    a.wait_ge(sq_added.sem, sq_added.at(L, base + j - 1))
                a.activation(sqr[:, j % 2, :], x[:, c, hs(h)], ACT.Square).then_inc(sq_made.sem, 1)

            def roots(L, i):
                for h in range(2):
                    a.wait_ge(aux_done.sem, aux_at(L, ("sum", i, h)))
                    a.activation(rt_c[:, 4 * h:4 * h + 4], aux[:, h, 0:4], ACT.Sqrt,
                                 bias=eps_c).then_inc(aux_emptied[h].sem, 1)

            def rows_out(L, i):
                for h in range(2):
                    a.wait_ge(aux_done.sem, aux_at(L, ("row", i, h)))
                    a.activation(rstd[:, h, :], aux[:, 2 + h, :], ACT.Copy).then_inc(aux_emptied[2 + h].sem, 1)

            def high_part(c, h, gain):
                a.activation(hh[:, c, hs(h)], x[:, c, hs(h)], ACT.Copy,
                             scale=gain).then_inc(h_hi.sem, 1)

            a.dma_start(early[:, :], early_d).then_inc(early_landed, 16)
            for h in range(2):
                a.dma_start(posi[64 * h:64 * h + 64, :],
                            pos_d[hs(h)].partition_broadcast(64)).then_inc(pos_landed, 16)
            for c in range(KC):
                a.dma_start(x[:, c, :], x_d[:, c, :]).then_inc(x_landed[c], 16)
            a.dma_start(const[:, :], const_d).then_inc(const_landed, 16)
            a.wait_ge(early_landed, 16)
            a.wait_ge(pre_vec, 4)
            for j in range(16):
                if j == 8:
                    a.wait_ge(pre_vec, PRE_VEC)
                    for i, table in enumerate((sinT, cosT)):
                        for h in range(2):
                            r = slice(64 * h, 64 * h + 64)
                            a.activation(table[r, hs(h)], ang[r, 1 + i, :], ACT.Sin).then_inc(pre_act, 1)
                    a.wait_ge(pre_act, 4)
                    for table in (sinT, cosT):
                        for h in range(2):
                            a.dma_start(table[64 - 64 * h:128 - 64 * h, hs(h)],
                                        table[64 * h:64 * h + 64, hs(h)]).then_inc(trig_spread, 16)
                square(0, -16, j, lambda c, h, j: a.wait_ge(x_landed[c], 16))

            T0, QR, KR, QX, VT, KZ, SC0 = rw
            by = "p (n c) -> p n c"

            with a.Fori(0, DEPTH) as L:
                a.wait_ge(gains_kept, L + 1)
                a.dma_start(par[:, :], par_d[L]).then_inc(par_landed, 16)
                a.dma_start(spill_d, x[:, :, :]).then_inc(spilled, 16)
                for item in MACRO:
                    what, args = item[0], item[1:]
                    if what == "norm":
                        a.wait_ge(unit_done.sem, unit_done.at(L, 0))
                        for j in range(16):
                            h, c = divmod(j, 8)
                            high_part(c, h, mix_gain[:, c:c + 1])
                        roots(L, 0)
                        rows_out(L, 0)
                    elif what == "unit":
                        u = args[0]
                        if u == U_MQ + 1:
                            a.wait_ge(vec_step.sem, mark_at(L, "neg_abs"))
                            a.activation(mix[0:MH, 3, :], mix[0:MH, 3, :], ACT.Exp).then_inc(row_act.sem, 1)
                            a.wait_ge(row_act.sem, row_act.at(L, 1))
                            a.activation(mix[0:MH, 3, :], mix[0:MH, 3, :], ACT.Ln,
                                         bias=one_c[0:MH]).then_inc(row_act.sem, 1)
                        if u == U_MV + 1:
                            a.wait_ge(vec_step.sem, mark_at(L, "inter_log"))
                            a.activation(mix[0:MH, 0, :], mix[0:MH, 1, :], ACT.Exp).then_inc(row_act.sem, 1)
                            a.wait_ge(vec_step.sem, mark_at(L, "m_row"))
                            a.activation(rows[96:96 + MH, 0, :], mix[0:MH, 4, :], ACT.Exp,
                                         scale=-1.0).then_inc(row_act.sem, 1)
                            a.wait_ge(vec_step.sem, mark_at(L, "pw_log"))
                            a.activation(rows[0:MH, 1, :], mix[0:MH, 3, :], ACT.Exp).then_inc(row_act.sem, 1)
                        if u == U_MV + 2:
                            for c in range(6):
                                a.wait_ge(vec_step.sem, mark_at(L, ("conv", c)))
                                a.activation(qk[:, c, :], qk[:, c, :], ACT.Silu).then_inc(silu_made.sem, 1)
                    elif what == "ml_cols":
                        for b in range(4):
                            a.wait_ge(aux_done.sem, aux_at(L, ("tt", b)))
                            src = abank(("tt", b)).rearrange("p (n q h) -> p n q h", n=2, q=8)
                            a.activation(tt[:, 2 * b:2 * b + 2, :, :], src[:, :, 0:5, 0:MH],
                                         ACT.Copy).then_inc(aux_emptied[b].sem, 1)
                        a.wait_ge(aux_done.sem, aux_at(L, ("so",)))
                        a.activation(so6.rearrange("p b n -> p (b n)"), abank(("so",))[:, 0:NB * NCH],
                                     ACT.Copy).then_inc(aux_emptied[0].sem, 1)
                    elif what == "ml_a":
                        n = args[0]
                        a.wait_ge(aux_done.sem, aux_at(L, ("tv", n)))
                        if n == 0:
                            a.wait_ge(vec_step.sem, mark_at(L, "vx_ones"))
                        a.activation(vx[:, n % 2, :, 0:MD], abank(("tv", n))[:, 0:MW].rearrange("p (h d) -> p h d", h=MH),
                                     ACT.Copy).then_inc(aux_emptied[1].sem, 1)
                        a.wait_ge(aux_read(("mb", n)), aux_read_at(L, ("mb", n)))
                        a.activation(dmat.rearrange("p h c -> p (h c)"), dmat.rearrange("p h c -> p (h c)"),
                                     ACT.Exp).then_inc(d_exp.sem, 1)
                    elif what == "gate_funcs":
                        for i, c in enumerate((5, 6, 7, 0, 1, 2)):
                            u = U_MO + i
                            a.wait_ge(emptied[bank(u, 0)].sem, emptied_at(L, u, 0))
                            a.wait_ge(emptied[bank(u, 1)].sem, emptied_at(L, u, 1))
                            a.activation(mix[:, c, :], mix[:, c, :], ACT.Sigmoid if i < 3 else ACT.Silu).then_inc(gated.sem, 1)
                        a.wait_ge(vec_step.sem, mark_at(L, ("ml_var", NCH - 1)))
                        a.activation(stat[:, :, :], stat[:, :, :], ACT.Sqrt, bias=eps_c,
                                     scale=1.0 / MD).then_inc(ml_rt.sem, 1)
                    elif what == "pool":
                        for j in range(2):
                            for h in range(2):
                                name = ("pm", j, h)
                                a.wait_ge(aux_done.sem, aux_at(L, name))
                                a.activation(mix[:, 3 + j, hs(h)], abank(name), ACT.Copy,
                                             scale=par[:, A_PS + j:A_PS + j + 1]).then_inc(aux_read(name), 1)
                    elif what == "turn":
                        p = args[0]
                        for h in range(2):
                            name = ("vt", p, h)
                            a.wait_ge(aux_done.sem, aux_at(L, name))
                            a.activation(VT[:, hs(h)], abank(name), ACT.Copy).then_inc(aux_read(name), 1)
                        if p == PAIRS - 1:
                            a.wait_ge(vec_step.sem, mark_at(L, ("cos_part", p, 0)))
                            a.dma_start(x[:, 0:3, :], spill_d[:, 0:3, :]).then_inc(reloaded[1], 16)
                    elif what == "ret_y":
                        p = args[0]
                        for h in range(2):
                            name = ("ry", p, h)
                            a.wait_ge(aux_done.sem, aux_at(L, name))
                            a.activation(KR[:, hs(h)], abank(name), ACT.Square).then_inc(ret_sq.sem, 1)
                            a.activation(T0[:, hs(h)], abank(name), ACT.Copy).then_inc(aux_read(name), 1)
                        if p == PAIRS - 1:
                            a.dma_start(x[:, 6:8, :], spill_d[:, 6:8, :]).then_inc(reloaded[2], 16)
                    elif what == "spread":
                        p = args[0]
                        for h in range(2):
                            name = ("rv", p, h)
                            a.wait_ge(aux_done.sem, aux_at(L, name))
                            a.activation(KZ[:, hs(h)], abank(name), ACT.Ln, bias=eps_c).then_inc(aux_read(name), 1)
                            a.wait_ge(aux_read(name), aux_read_at(L, name))
                            a.activation(KZ[:, hs(h)], KZ[:, hs(h)], ACT.Exp, scale=-0.5).then_inc(ret_rstd.sem, 1)
                    elif what == "early_high":
                        a.dma_start(x[:, 3:6, :], spill_d[:, 3:6, :]).then_inc(reloaded[0], 16)
                        a.wait_ge(unit_done.sem, unit_done.at(L, U_OUT))
                        for i in range(14):
                            h, c = i // 7, EARLY[i % 7]
                            if c < 3:
                                a.wait_ge(vec_step.sem, mark_at(L, ("ret_mix", c, h)))
                            elif c < 5:
                                a.wait_ge(aux_read(("pm", c - 3, h)), aux_read_at(L, ("pm", c - 3, h)))
                            else:
                                a.wait_ge(aux_read(("yt", c - 5, h)), aux_read_at(L, ("yt", c - 5, h)))
                            a.activation(hh[:, c, hs(h)], mix[:, c, hs(h)], ACT.Copy).then_inc(h_hi.sem, 1)
                    elif what == "mix_split":
                        c = MIX_ORDER[7]
                        for h in range(2):
                            a.wait_ge(vec_step.sem, mark_at(L, ("ret_mix", c, h)))
                            a.activation(hh[:, c, hs(h)], mix[:, c, hs(h)], ACT.Copy).then_inc(h_hi.sem, 1)
                        a.dma_start(praw[:, :, :], p_d[L]).then_inc(p_landed, 16)
                    elif what == "out_units":
                        for j in range(16):
                            square(L, 0, j, lambda c, h, j: a.wait_ge(emptied[bank(U_OUT + c, h)].sem,
                                                                      emptied_at(L, U_OUT + c, h)))
                            if j >= 14:
                                for c in range(KC):
                                    high_part(c, j - 14, par[:, A_FFN + c:A_FFN + c + 1])
                        roots(L, 1)
                        a.wait_ge(p_landed, L * 16 + 16)
                        for k in range(2):
                            a.activation(phi[:, k, :], praw[:, k, :], ACT.Copy).then_inc(p_hi_made.sem, 1)
                        rows_out(L, 1)
                    elif what == "ffn":
                        def ffn_up(u, g, lp):
                            for f in range(2):
                                ug = u + 2 * f
                                for h in range(2):
                                    a.wait_ge(emptied[bank(ug, h)].sem, emptied_at(L, ug, h, lp.fills))
                                    a.activation(silu_g[:, h, :], silu_g[:, h, :],
                                                 ACT.Silu).then_inc(ffn_silu.sem, 1)
                                for h in range(2):
                                    a.wait_ge(act_made.sem, act_made.at(L, lp.acts + (4 * g + 2 * f + h + 1)))
                                    a.activation(ahi[:, g % 2, f, hs(h)], act_t[:, h, :],
                                                 ACT.Copy).then_inc(act_hi_made.sem, 1)

                        ffn_up(U_FFN, 0, LoopValues(0))
                        with a.Fori(0, FG // 2) as i:
                            lp = LoopValues(i)
                            ffn_up(U_FFN + 4, 1, lp)
                            ffn_up(U_FFN + 10, 2, lp)
                        for j in range(16):
                            square(L, 16, j, lambda c, h, j: a.wait_ge(emptied[bank(U_PROJ - 2 + j // 8, j % 8)].sem,
                                                                       emptied_at(L, U_PROJ - 2 + j // 8, j % 8)))
                            high_part(j // 2, j % 2, par[:, A_PLE + j // 2:A_PLE + j // 2 + 1])
                    elif what == "ple_proj":
                        def out(k):
                            u, kk = U_PROJ + k // 8, k % 8
                            a.wait_ge(filled(u, kk), filled_at(L, u, kk))
                            a.activation(pp[:, k // 2, hs(k % 2)], pbank(u, kk),
                                         ACT.Copy).then_inc(emptied[bank(u, kk)].sem, 1)
                        a.activation(mix_gain, par[:, A_NEXT:A_NEXT + KC], ACT.Copy).then_inc(gains_kept, 1)
                        for k in range(8):
                            out(k)
                        roots(L, 2)
                        for k in range(8, 12):
                            out(k)
                        rows_out(L, 2)
                        for k in range(12, 16):
                            out(k)
                    elif what == "ple_gate":
                        for j in range(16 + 1):
                            if j < 16:
                                m, h = divmod(j, 2)
                                a.wait_ge(emptied[bank(U_GATE + m, h)].sem, emptied_at(L, U_GATE + m, h))
                                a.activation(psg[:, h, :], psg[:, h, :], ACT.Sigmoid).then_inc(ple_sig.sem, 1)
                            if j >= 1:
                                square(L, 32, j - 1, lambda c, h, jj: a.wait_ge(x_ple.sem, x_ple.at(L, jj + 1)))
            roots(DEPTH, 0)
            rows_out(DEPTH, 0)
            for j in range(16):
                h, c = divmod(j, 8)
                a.wait_ge(result, j + 1)
                a.dma_start(out_d[:, c, hs(h)], x[:, c, hs(h)]).then_inc(out_stored, 16)
            a.wait_ge(out_stored, 16 * 16)

        @block.sync
        def _(sp):
            with sp.Fori(0, DEPTH * UNITS // (RAW * RING)) as i:
                for r in range(RAW * RING):
                    sp.wait_ge(weights_ready.sem, i * (RAW * RING) + (r + RING + 1 - RAW))
                    sp.dma_start(raw[:, r % RAW, :], w_d[i * (RAW * RING) + r]).then_inc(raw_landed[r % RAW], 16)

        @block.gpsimd
        def _(g):
            g.memset(zero1[:, :], 0.0).then_inc(w_hi_made, 1)
            g.sem_inc(weights_ready.sem, RING)
            g.wait_ge(w_hi_made, 1)
            with g.Fori(0, DEPTH * UNITS // (RAW * RING)) as i:
                for r in range(RAW * RING):
                    w, slot = raw[:, r % RAW, :], r % RING
                    g.wait_ge(unit_done.sem, i * (RAW * RING) + (r + 1))
                    g.wait_ge(raw_landed[r % RAW], i * (16 * RING) + 16 * (r // RAW + 1))
                    g.tensor_tensor(whi[:, slot, :], w, zero1[:, 0:1].to_broadcast([P, 1024]),
                                    ALU.add).then_inc(w_hi_made, 1)
                    g.wait_ge(w_hi_made, i * (RAW * RING) + (r + 2))
                    g.tensor_tensor(wlo[:, slot, :], w, whi[:, slot, :].bitcast(F32),
                                    ALU.subtract).then_inc(weights_ready.sem, 1)

        @block.tensor
        def _(pe):
            pe.sem_inc(unit_done.sem, RING)
            T0, QR, KR, QX, VT, KZ, SC0 = rw

            def three_passes(out, slot, col, rhi, rlo, first, final):
                wh, wl = whi[:, slot, col:col + P], wlo[:, slot, col:col + P]
                pe.matmul(out, wh, rhi, start=first, stop=False)
                pe.matmul(out, wl, rhi, start=False, stop=False)
                return pe.matmul(out, wh, rlo, start=False, stop=final)

            def product(out, u, slot_w, col, ks, rhi, rlo, ready=None):
                last = None
                for i, (k, wk) in enumerate(ks):
                    if ready is not None:
                        ready(i, k)
                    last = three_passes(out, slot_w, wk + col, rhi(k), rlo(k), i == 0, i == len(ks) - 1)
                return last

            def tell(ins, u, k):
                ins.then_inc(unit_done.sem if k == unit_fills(u) - 1 else fill_done.sem, 1)

            def narrow(L, u, h, order=range(KC), ready=None, fills=0, units=0):
                if h == 0:
                    pe.wait_ge(weights_ready.sem, weights_ready.at(L, units + (u + 1)))
                pe.wait_ge(emptied[bank(u, h)].sem, free_at(L, u, h, fills))
                tell(product(pbank(u, h), u, u % RING, 0, [(k, P * k) for k in order],
                             lambda k: hh[:, k, hs(h)], lambda k: hl[:, k, hs(h)], ready), u, h)

            def wide(L, u, k, rhi, rlo, fills=0, units=0):
                if k == 0:
                    pe.wait_ge(weights_ready.sem, weights_ready.at(L, units + (u + 1)))
                pe.wait_ge(emptied[bank(u, k)].sem, free_at(L, u, k, fills))
                m, h = divmod(k, 2)
                tell(product(pbank(u, k), u, u % RING, P * m, [(0, 0), (1, HALF)],
                             lambda c: rhi[:, c, hs(h)], lambda c: rlo[:, c, hs(h)]), u, k)

            def sums(L, base, i):
                for h in range(2):
                    pe.wait_ge(sq_added.sem, sq_added.at(L, base + 15 + h))
                    pe.wait_ge(aux_read(("sum", i, h)), aux_free_at(L, ("sum", i, h)))
                    for t in range(4):
                        ins = pe.matmul(aux[:, h, t:t + 1], acc[:, h, P * t:P * t + P], const[:, C_PART:C_PART + 1],
                                        start=True, stop=True)
                    ins.then_inc(aux_done.sem, 1)

            def spread_rstd(L, i):
                for h in range(2):
                    pe.wait_ge(diag_made.sem, diag_made.at(L, 2 * i + h + 1))
                    pe.wait_ge(aux_read(("row", i, h)), aux_free_at(L, ("row", i, h)))
                    pe.matmul(aux[:, 2 + h, :], ones, diag.rearrange("p t c -> p (t c)"),
                              start=True, stop=True).then_inc(aux_done.sem, 1)

            pe.wait_ge(const_landed, 16)

            with pe.Fori(0, DEPTH) as L:
                for item in MACRO:
                    what, args = item[0], item[1:]
                    if what == "unit":
                        u = args[0]
                        for h in range(2):
                            ready = None
                            if u == U_GATES:
                                ready = lambda i, k, h=h: pe.wait_ge(h_ready.sem, h_ready.at(L, 8 * h + k + 1))
                            narrow(L, u, h, ready=ready)
                            if h == 0 and u == U_GATES:
                                sums(L, -16, 0)
                            if h == 0 and u == U_GATES + 1:
                                spread_rstd(L, 0)
                    elif what == "half":
                        narrow(L, *args)
                    elif what == "ml_cols":
                        pe.wait_ge(vec_step.sem, mark_at(L, "rows_end"))
                        pe.wait_ge(row_act.sem, row_act.at(L, 5))
                        for b in range(4):
                            pe.wait_ge(aux_read(("tt", b)), aux_free_at(L, ("tt", b)))
                            for n in (2 * b, 2 * b + 1):
                                for s in range(2):
                                    o = (n % 2) * 256 + s * P
                                    ins = pe.transpose(abank(("tt", b))[:, o:o + P], rows[:, s, P * n:P * n + P], ident)
                            ins.then_inc(aux_done.sem, 1)
                        pe.wait_ge(aux_read(("so",)), aux_free_at(L, ("so",)))
                        for i, (h, *_) in enumerate(BLOCKS):
                            ins = pe.matmul(abank(("so",))[:, NCH * i:NCH * i + NCH],
                                            const[32:32 + MH, C_SEL + P * h:C_SEL + P * h + P],
                                            rows[32:32 + MH, 1, 0:NCH], start=True, stop=True)
                        ins.then_inc(aux_done.sem, 1)
                    elif what == "ml_a":
                        n = args[0]
                        cs = slice(P * n, P * n + P)
                        if n == 0:
                            pe.wait_ge(silu_made.sem, silu_made.at(L, 6))
                            for u in range(U_MV, U_MO):
                                pe.wait_ge(emptied[bank(u, 0)].sem, emptied_at(L, u, 0))
                                pe.wait_ge(emptied[bank(u, 1)].sem, emptied_at(L, u, 1))
                        pe.wait_ge(aux_read(("tk", n)), aux_free_at(L, ("tk", n)))
                        for j in range(MC):
                            ins = pe.transpose(abank(("tk", n))[:, P * j:P * j + P], qk[:, 3 + j, cs], ident)
                        ins.then_inc(aux_done.sem, 1)
                        pe.wait_ge(aux_read(("tv", n)), aux_free_at(L, ("tv", n)))
                        for j in range(MC):
                            ins = pe.transpose(abank(("tv", n))[:, P * j:P * j + P], vm[:, n, P * j:P * j + P], ident)
                        ins.then_inc(aux_done.sem, 1)
                        pe.wait_ge(aux_read(("mb", n)), aux_free_at(L, ("mb", n)))
                        for h in range(MH):
                            ins = pe.matmul(abank(("mb", n))[:, P * h:P * h + P],
                                            const[32:32 + MH, C_SEL + P * h:C_SEL + P * h + P],
                                            rows[32:32 + MH, 0, cs], start=True, stop=True)
                        ins.then_inc(aux_done.sem, 1)
                        pe.wait_ge(aux_read(("ms", n)), aux_free_at(L, ("ms", n)))
                        pe.wait_ge(vec_step.sem, mark_at(L, ("key_blocks", n)))
                        for b, (h, j, *_) in enumerate(BLOCKS):
                            ins = pe.matmul(abank(("ms", n))[:, P * h:P * h + P], km[:, n % 2, b, :], qk[:, j, cs],
                                            start=b == 0 or BLOCKS[b - 1][0] != h,
                                            stop=b == NB - 1 or BLOCKS[b + 1][0] != h)
                        ins.then_inc(aux_done.sem, 1)
                    elif what == "ml_b":
                        n = args[0]
                        cs, E = slice(P * n, P * n + P), MD + 1
                        pe.wait_ge(aux_read(("ms", n)), aux_read_at(L, ("ms", n)))
                        pe.wait_ge(aux_read(("tv", n)), aux_read_at(L, ("tv", n)))
                        pe.wait_ge(aux_read(("num", n)), aux_free_at(L, ("num", n)))
                        for h in range(MH):
                            ins = pe.matmul(abank(("num", n))[:, E * h:E * h + E], smat[:, h, :], vx[:, n % 2, h, :],
                                            start=True, stop=True)
                        ins.then_inc(aux_done.sem, 1)
                        if n > 0:
                            pe.wait_ge(aux_read(("kv0", n - 1)), aux_read_at(L, ("kv0", n - 1)))
                            pe.wait_ge(aux_read(("kv1", n - 1)), aux_read_at(L, ("kv1", n - 1)))
                        else:
                            pe.wait_ge(vec_step.sem, mark_at(L, "c_zero"))
                        pe.wait_ge(aux_read(("int", n)), aux_free_at(L, ("int", n)))
                        for b, (h, j, *_) in enumerate(BLOCKS):
                            ins = pe.matmul(abank(("int", n))[:, E * h:E * h + E], qk[:, j, cs], cst[:, n % 2, b, :],
                                            start=b == 0 or BLOCKS[b - 1][0] != h,
                                            stop=b == NB - 1 or BLOCKS[b + 1][0] != h)
                        ins.then_inc(aux_done.sem, 1)
                        if n < NCH - 1:
                            pe.wait_ge(vec_step.sem, mark_at(L, ("kw_first", n)))
                            pe.wait_ge(aux_read(("tk", n)), aux_read_at(L, ("tk", n)))
                            for i in range(2):
                                pe.wait_ge(aux_read((f"kv{i}", n)), aux_free_at(L, (f"kv{i}", n)))
                                for b in range(3):
                                    h = BLOCKS[3 * i + b][0]
                                    ins = pe.matmul(abank((f"kv{i}", n))[:, E * b:E * b + E], kw[:, 3 * i + b, :],
                                                    vx[:, n % 2, h, :], start=True, stop=True)
                                ins.then_inc(aux_done.sem, 1)
                    elif what == "ml_fin":
                        for j in range(MC):
                            for h in range(2):
                                name = ("yt", j, h)
                                pe.wait_ge(vec_step.sem, mark_at(L, ("ml_y", 4 * h + 3)))
                                pe.wait_ge(aux_read(name), aux_free_at(L, name))
                                for n in range(4):
                                    ins = pe.transpose(abank(name)[:, P * n:P * n + P], vm[:, 4 * h + n, P * j:P * j + P], ident)
                                ins.then_inc(aux_done.sem, 1)
                    elif what == "pool":
                        for j in range(2):
                            pe.wait_ge(vec_step.sem, mark_at(L, ("pooled", j)))
                            for h in range(2):
                                name = ("pm", j, h)
                                pe.wait_ge(aux_read(name), aux_free_at(L, name))
                                pe.matmul(abank(name), par[:, A_PW + P * j:A_PW + P * j + P],
                                                   mix[:, 3 + j, hs(h)], start=True, stop=True).then_inc(aux_done.sem, 1)
                    elif what == "rope":
                        p = args[0]
                        for w, nm in ((1, "pk"), (0, "pq")):
                            for h in range(2):
                                pe.wait_ge(emptied[bank(U_RET + 3 * p + w, h)].sem, emptied_at(L, U_RET + 3 * p + w, h))
                                pe.wait_ge(aux_read((nm, p, h)), aux_free_at(L, (nm, p, h)))
                                pe.matmul(abank((nm, p, h)), const[:, C_PERM:C_PERM + P],
                                                   rqkv[:, p % 2, w, hs(h)], start=True, stop=True).then_inc(aux_done.sem, 1)
                    elif what == "turn":
                        p = args[0]
                        for h in range(2):
                            name = ("kz", p, h)
                            pe.wait_ge(vec_step.sem, mark_at(L, ("roped", p, 1, h)))
                            pe.wait_ge(aux_read(name), aux_free_at(L, name))
                            for n in range(4):
                                o = HALF * h + P * n
                                ins = pe.transpose(abank(name)[:, P * n:P * n + P], KR[:, o:o + P], ident)
                            ins.then_inc(aux_done.sem, 1)
                        for h in range(2):
                            name = ("vt", p, h)
                            pe.wait_ge(emptied[bank(U_RET + 3 * p + 2, h)].sem, emptied_at(L, U_RET + 3 * p + 2, h))
                            pe.wait_ge(aux_read(name), aux_free_at(L, name))
                            for n in range(4):
                                o = HALF * h + P * n
                                ins = pe.matmul(abank(name)[:, P * n:P * n + P], rqkv[:, p % 2, 2, o:o + P],
                                                const[:, C_CEN:C_CEN + P], start=True, stop=True)
                            ins.then_inc(aux_done.sem, 1)
                    elif what == "scores":
                        p = args[0]
                        pe.wait_ge(vec_step.sem, mark_at(L, ("roped", p, 0, 1)))
                        for e in range(2):
                            r = slice(RD * e, RD * e + RD)
                            for h in range(2):
                                name = ("rs", p, e, h)
                                pe.wait_ge(aux_read(name), aux_free_at(L, name))
                                for n in range(4):
                                    o = HALF * h + P * n
                                    ins = pe.matmul(abank(name)[:, P * n:P * n + P], KR[r, o:o + P], QR[r, o:o + P],
                                                    start=True, stop=True)
                                ins.then_inc(aux_done.sem, 1)
                    elif what == "state":
                        p = args[0]
                        name = ("rkv", p)
                        pe.wait_ge(aux_read(("vt", p, 1)), aux_read_at(L, ("vt", p, 1)))
                        pe.wait_ge(aux_read(("kz", p, 1)), aux_read_at(L, ("kz", p, 1)))
                        pe.wait_ge(aux_read(name), aux_free_at(L, name))
                        for n in range(NCH):
                            for e in range(2):
                                o = P * n + RD * e
                                ins = pe.matmul(abank(name)[RD * e:RD * e + RD, RD * n:RD * n + RD], KZ[:, o:o + RD],
                                                VT[:, o:o + RD], start=True, stop=True)
                        ins.then_inc(aux_done.sem, 1)
                    elif what == "ret_y":
                        p = args[0]
                        pe.wait_ge(vec_step.sem, mark_at(L, ("q_xi", p)))
                        for h in range(2):
                            name = ("ry", p, h)
                            pe.wait_ge(aux_read(("rs", p, 0, h)), aux_read_at(L, ("rs", p, 0, h)))
                            pe.wait_ge(aux_read(("rs", p, 1, h)), aux_read_at(L, ("rs", p, 1, h)))
                            pe.wait_ge(aux_read(("rkv", p)), aux_read_at(L, ("rkv", p)))
                            pe.wait_ge(aux_read(name), aux_free_at(L, name))
                            for n in range(4 * h, 4 * h + 4):
                                for e in range(2):
                                    r = slice(RD * e, RD * e + RD)
                                    out = abank(name)[r, P * (n % 4):P * (n % 4) + P]
                                    s = SC0[:, P * n:P * n + P] if e == 0 else sc1[:, n, :]
                                    pe.matmul(out, VT[:, P * n + RD * e:P * n + RD * e + RD], s, start=True, stop=False)
                                    ins = pe.matmul(out, rst[r, n, :], QX[r, P * n:P * n + P], start=False, stop=True)
                            ins.then_inc(aux_done.sem, 1)
                    elif what == "spread":
                        p = args[0]
                        for h in range(2):
                            name = ("rv", p, h)
                            pe.wait_ge(ret_sq.sem, ret_sq.at(L, 2 * p + h + 1))
                            pe.wait_ge(aux_read(name), aux_free_at(L, name))
                            pe.matmul(abank(name), const[:, C_MEAN:C_MEAN + P], KR[:, hs(h)], start=True, stop=True).then_inc(aux_done.sem, 1)
                    elif what == "out_part":
                        m, h = divmod(args[0], 2)
                        u = U_OUT + m
                        if h == 0:
                            pe.wait_ge(weights_ready.sem, weights_ready.at(L, u + 1))
                        pe.wait_ge(emptied[bank(u, h)].sem, free_at(L, u, h))
                        for i, c in enumerate(EARLY):
                            if m == 0:
                                pe.wait_ge(h_ready.sem, h_ready.at(L, 16 + 7 * h + i + 1))
                            three_passes(pbank(u, h), u % RING, P * c, hh[:, c, hs(h)], hl[:, c, hs(h)], i == 0, False)
                    elif what == "out_units":
                        c = MIX_ORDER[7]
                        for k in range(4):
                            m, h = divmod(k, 2)
                            if m == 0:
                                pe.wait_ge(h_ready.sem, h_ready.at(L, 16 + 14 + h + 1))
                            ins = three_passes(pbank(U_OUT + m, h), (U_OUT + m) % RING, P * c, hh[:, c, hs(h)],
                                               hl[:, c, hs(h)], False, True)
                            ins.then_inc(filled(U_OUT + m, h), 1)
                        for m in range(2, 8):
                            for h in range(2):
                                narrow(L, U_OUT + m, h)
                    elif what == "ffn":
                        def up(u, g, lp, first=False):
                            for f in range(4):
                                for h in range(2):
                                    ready = None
                                    if first and f == 0:
                                        ready = lambda i, k, h=h: pe.wait_ge(h_ready.sem, h_ready.at(L, 32 + 8 * h + k + 1))
                                    narrow(L, u + f, h, ready=ready, fills=lp.fills, units=lp.units)
                                    if first and f == 0:
                                        if h == 0:
                                            sums(L, 0, 1)
                                    if first and f == 1 and h == 0:
                                        spread_rstd(L, 1)

                        def down(u, g, lp):
                            pe.wait_ge(act_ready.sem, act_ready.at(L, lp.acts + (4 * g + 4)))
                            for k in range(16):
                                wide(L, u + k // 8, k % 8, ahi[:, g % 2], alo[:, g % 2], lp.fills, lp.units)

                        up(U_FFN, 0, LoopValues(0), True)
                        with pe.Fori(0, FG // 2) as i:
                            lp = LoopValues(i)
                            up(U_FFN + 4, 1, lp)
                            down(U_FFN + 8, 0, lp)
                            up(U_FFN + 10, 2, lp)
                            down(U_FFN + 14, 1, lp)
                        down(U_PROJ - 2, FG - 1, LoopValues(0))
                    elif what == "ple_proj":
                        pe.wait_ge(p_ready.sem, p_ready.at(L, 2))
                        for k in range(16):
                            wide(L, U_PROJ + k // 8, k % 8, phi[:, :, :], plo[:, :, :])
                            if k == 7:
                                sums(L, 16, 2)
                            if k == 11:
                                spread_rstd(L, 2)
                    elif what == "ple_gate":
                        for m in range(8):
                            for h in range(2):
                                ready = None
                                if m == 0:
                                    ready = lambda i, k, h=h: pe.wait_ge(h_ready.sem, h_ready.at(L, 48 + 8 * h + k + 1))
                                narrow(L, U_GATE + m, h, ready=ready)
            sums(DEPTH, -16, 0)
            spread_rstd(DEPTH, 0)


def constants():
    c = np.zeros((P, C_ALL), np.float64)
    i = np.arange(P)
    c[:, C_ID:C_ID + P] = np.eye(P)
    c[:, C_ONE:C_ONE + P] = 1.0
    for m in range(P):
        if m % RD < RD // 2:
            c[m + RD // 2, C_PERM + m] = -1.0
        else:
            c[m - RD // 2, C_PERM + m] = 1.0
    same = (i[:, None] // RD == i[None, :] // RD) / float(RD)
    c[:, C_CEN:C_CEN + P] = np.eye(P) - same
    c[:, C_MEAN:C_MEAN + P] = same
    c[:, C_NEG:C_NEG + P] = np.where(i[:, None] <= i[None, :], 0.0, -1e30)
    gamma = 1.0 - 2.0 ** (-5.0 - np.arange(RH))
    for h in range(RH):
        rel = i[None, :] - i[:, None]
        c[:, C_DEC + P * h:C_DEC + P * h + P] = np.where(rel >= 0, RSCALE * gamma[h] ** np.maximum(rel, 0), 0.0)
        c[:, C_ZETA + h] = RSCALE * gamma[h] ** (CHUNK - 1 - i)
    for p in range(PAIRS):
        g = gamma[2 * p + i // RD]
        c[:, C_XI + P * p:C_XI + P * p + P] = g[:, None] ** (i[None, :] + 1)
        c[:, C_GAM + p] = g ** CHUNK
    for h in range(MH):
        c[32 + h, C_SEL + P * h:C_SEL + P * h + P] = 1.0
    for j in range(2):
        w = np.array([2.0, 4.0, 8.0, 16.0])[2 * j + i // 64]
        c[:, C_INVC + 16 * j:C_INVC + 16 * j + 16] = 1.0 / np.minimum(np.arange(1, 17)[None, :], w[:, None])
        c[:, C_INVW + j] = 1.0 / w
    c[:, C_PART] = 1.0 / D
    for b, (_, _, first, last) in enumerate(BLOCKS):
        c[first:last, C_BLK + b] = 1.0
    return c.astype(np.float32)


def by_partition(a):
    return np.ascontiguousarray(np.moveaxis(a.reshape((-1, P) + a.shape[1:]), 0, 1))


def pack_weights(w_in, w_out, w_gate_up, w_down, w_ple_gate, w_ple_proj):
    out = np.zeros((UNITS, P, 1024), np.float32)

    def narrow(u, w, col):
        out[u] = by_partition(w[:, col:col + P]).reshape(P, 1024)

    def wide(u, w, row, col):
        out[u] = by_partition(w[row:row + 2 * P, col:col + HALF]).reshape(P, 1024)

    rq, rk, rv, rg, pu, mq, mk, mv, mo, mi, mf = np.cumsum([0] + [RW] * 4 + [PW] + [MW] * 4 + [MH])
    gates = out[U_GATES].reshape(P, KC, P)
    gates[:, :, 0:MH] = by_partition(w_in[:, mi:mi + MH])
    gates[:, :, 32:32 + MH] = by_partition(w_in[:, mf:mf + MH])
    for u0, o in ((U_MQ, mq), (U_MK, mk), (U_MV, mv), (U_MO, mo), (U_RG, rg)):
        for j in range(3):
            narrow(u0 + j, w_in, o + P * j)
    for j in range(2):
        narrow(U_POOL + j, w_in, pu + P * j)
    for p in range(PAIRS):
        for w, o in enumerate((rq, rk, rv)):
            narrow(U_RET + 3 * p + w, w_in, o + P * p)
    for m in range(8):
        narrow(U_OUT + m, w_out, P * m)
        narrow(U_GATE + m, w_ple_gate, P * m)

    def up(u, g):
        for f in range(2):
            narrow(u + 2 * f, w_gate_up, P * (2 * g + f))
            narrow(u + 2 * f + 1, w_gate_up, DFF + P * (2 * g + f))

    def down(u, g):
        for m in range(2):
            wide(u + m, w_down, 2 * P * g, HALF * m)

    up(U_FFN, 0)
    for g in range(1, FG):
        up(U_FFN + 6 * g - 2, g)
        down(U_FFN + 6 * g + 2, g - 1)
    down(U_PROJ - 2, FG - 1)
    for m in range(2):
        wide(U_PROJ + m, w_ple_proj, 0, HALF * m)
    return out


def kernel(x, p, positions, norm_mix, w_in, ret_gn, pool_w, pool_scale, conv_w, conv_b, b_igate, b_fgate,
           mlstm_gn, w_out, norm_ffn, w_gate_up, w_down, norm_ple, w_ple_gate, w_ple_proj, norm_final):
    import concourse.bacc as bacc
    from concourse.bass_utils import run_bass_kernel_spmd

    f = lambda a: np.asarray(a)
    weights = np.concatenate([pack_weights(f(w_in)[i], f(w_out)[i], f(w_gate_up)[i], f(w_down)[i],
                                           f(w_ple_gate)[i], f(w_ple_proj)[i]) for i in range(DEPTH)])
    par = np.zeros((DEPTH, P, A_ALL), np.float32)
    for i in range(DEPTH):
        par[i, :, A_FFN:A_FFN + 8] = by_partition(f(norm_ffn)[i])
        par[i, :, A_PLE:A_PLE + 8] = by_partition(f(norm_ple)[i])
        after = f(norm_mix)[i + 1] if i + 1 < DEPTH else f(norm_final)
        par[i, :, A_NEXT:A_NEXT + 8] = by_partition(after)
        par[i, :, A_CW:A_CW + 6 * CONV] = by_partition(f(conv_w)[i].T).reshape(P, 6 * CONV)
        par[i, :, A_CB:A_CB + 6] = by_partition(f(conv_b)[i])
        par[i, 0:MH, A_GB] = f(b_igate)[i]
        par[i, 32:32 + MH, A_GB] = f(b_fgate)[i]
        par[i, :, A_RG:A_RG + PAIRS] = by_partition(f(ret_gn)[i])
        par[i, :, A_PS:A_PS + 2] = by_partition(f(pool_scale)[i])
        par[i, :, A_MG:A_MG + MC] = by_partition(f(mlstm_gn)[i])
        for g in range(4):
            j, e = divmod(g, 2)
            par[i, 64 * e:64 * e + 64, A_PW + P * j + 64 * e:A_PW + P * j + 64 * e + 64] = f(pool_w)[i, g]
    half = RD // 2
    frequencies = (10000.0 ** (-(np.arange(P)[:, None] % half) / half)).astype(np.float32)
    arrays = {
        "weights": weights,
        "x_in": by_partition(np.ascontiguousarray(f(x)[0].T)),
        "p_in": np.stack([by_partition(np.ascontiguousarray(f(p)[i, 0].T)) for i in range(DEPTH)]),
        "positions_in": np.ascontiguousarray(f(positions)[0]),
        "constants": constants(),
        "parameters": par,
        "early_in": np.concatenate([by_partition(f(norm_mix)[0]), frequencies], axis=1),
    }
    nc = bacc.Bacc("TRN2", target_bir_lowering=False, num_devices=1, dynamic_dma_scratch_size=1024)
    args = [nc.dram_tensor(n, a.shape, mybir.dt.from_np(a.dtype), kind="ExternalInput").ap() for n, a in arrays.items()]
    out = nc.dram_tensor("out", (P, KC, S), F32, kind="ExternalOutput").ap()
    build(nc, *args, out)
    r = run_bass_kernel_spmd(nc, [arrays], core_ids=[0])
    y = np.asarray(r.results[0]["out"])
    return np.ascontiguousarray(y.transpose(1, 0, 2).reshape(D, S).T)[None]
```
